# Optimizing a Trainium2 kernel written in Bass

```python
import jax
import jax.numpy as jnp
from jax import lax
import numpy as np

D_MODEL = 1024
BATCH = 1
SEQ = 256
DEPTH = 2

N_META = 16
M_HEADS = 4
M_DQK = 128
M_DV = D_MODEL // M_HEADS
CHUNK = 64
PAD_FRONT = CHUNK - N_META
CONV_WIDTH = D_MODEL
CONV_K = 3
N_GROUPS = 4
EXP_PER_GROUP = 4
N_EXPERTS = N_GROUPS * EXP_PER_GROUP
TOP_K = 2
D_EXPERT = 256
EPS = 1e-6
F_BIAS = 3.0
QK_W = M_HEADS * M_DQK
V_W = M_HEADS * M_DV
IN_WIDTHS = (QK_W, QK_W, V_W, M_HEADS, M_HEADS, V_W, CONV_WIDTH, CONV_WIDTH, CONV_WIDTH, CONV_WIDTH)
IN_TOTAL = sum(IN_WIDTHS)

kernel_name = 'hybrid_mlstm_shortconv_hmoe'

def rmsnorm(x, g):
    xf = x.astype(jnp.float32)
    y = xf * lax.rsqrt(jnp.mean(xf * xf, axis=-1, keepdims=True) + EPS)
    return (y * g.astype(jnp.float32)).astype(x.dtype)

def mlstm_chunkwise(q, k, v, ig, lf):
    Bsz, H, T, Dqk = q.shape
    Dv = v.shape[-1]
    nc = T // CHUNK

    def to_chunks(a):
        a = a.reshape((Bsz, H, nc, CHUNK) + a.shape[3:])
        return jnp.moveaxis(a, 2, 0)

    causal = jnp.tril(jnp.ones((CHUNK, CHUNK), dtype=bool))

    def step(carry, xs):
        C, n, m = carry
        qc, kc, vc, ic, fc = xs
        b = jnp.cumsum(fc, axis=-1)
        log_d = b[..., :, None] - b[..., None, :] + ic[..., None, :]
        log_d = jnp.where(causal, log_d, -jnp.inf)
        inter = b + m[..., None]
        m_t = jnp.maximum(inter, jnp.max(log_d, axis=-1))
        dmat = jnp.exp(log_d - m_t[..., None])
        s = jnp.einsum('bhtd,bhsd->bhts', qc, kc) * dmat
        e_inter = jnp.exp(inter - m_t)
        num = jnp.einsum('bhts,bhsv->bhtv', s, vc) + e_inter[..., None] * jnp.einsum('bhtd,bhdv->bhtv', qc, C)
        den = jnp.sum(s, axis=-1) + e_inter * jnp.einsum('bhtd,bhd->bht', qc, n)
        h = num / jnp.maximum(jnp.abs(den), jnp.exp(-m_t))[..., None]
        bL = b[..., -1]
        log_w = bL[..., None] - b + ic
        m_new = jnp.maximum(bL + m, jnp.max(log_w, axis=-1))
        w = jnp.exp(log_w - m_new[..., None])
        decay = jnp.exp(bL + m - m_new)
        C = decay[..., None, None] * C + jnp.einsum('bhs,bhsd,bhsv->bhdv', w, kc, vc)
        n = decay[..., None] * n + jnp.einsum('bhs,bhsd->bhd', w, kc)
        return (C, n, m_new), h

    init = (jnp.zeros((Bsz, H, Dqk, Dv), jnp.float32),
            jnp.zeros((Bsz, H, Dqk), jnp.float32),
            jnp.zeros((Bsz, H), jnp.float32))
    _, hs = lax.scan(step, init, (to_chunks(q), to_chunks(k), to_chunks(v), to_chunks(ig), to_chunks(lf)))
    return jnp.moveaxis(hs, 0, 2).reshape(Bsz, H, T, Dv)

def hybrid_mixer(h, w_in, b_if, conv_w, mh_gain, w_out):
    Bsz, L, _ = h.shape
    f32 = jnp.float32
    split_at = [int(s) for s in np.cumsum(IN_WIDTHS)[:-1]]
    q, k, v, ig, fg, g_m, cx, cb, cc, g_c = jnp.split(h @ w_in, split_at, axis=-1)

    def heads(a, d):
        return a.reshape(Bsz, L, M_HEADS, d).transpose(0, 2, 1, 3).astype(f32)

    q = heads(q, M_DQK) * (M_DQK ** -0.5)
    k = heads(k, M_DQK)
    v = heads(v, M_DV)
    ig = (ig.astype(f32) + b_if[:M_HEADS].astype(f32)).transpose(0, 2, 1)
    lf = jax.nn.log_sigmoid(fg.astype(f32) + b_if[M_HEADS:].astype(f32)).transpose(0, 2, 1)
    pad4 = ((0, 0), (0, 0), (PAD_FRONT, 0), (0, 0))
    pad3 = ((0, 0), (0, 0), (PAD_FRONT, 0))
    hm = mlstm_chunkwise(jnp.pad(q, pad4), jnp.pad(k, pad4), jnp.pad(v, pad4),
                         jnp.pad(ig, pad3, constant_values=-jnp.inf),
                         jnp.pad(lf, pad3))[:, :, PAD_FRONT:]
    hm = hm * lax.rsqrt(jnp.mean(hm * hm, axis=-1, keepdims=True) + EPS)
    hm = hm.transpose(0, 2, 1, 3).reshape(Bsz, L, V_W) * mh_gain.astype(f32)
    y_m = jax.nn.sigmoid(g_m.astype(f32)) * hm

    u = cc * cx
    up = jnp.pad(u, ((0, 0), (CONV_K - 1, 0), (0, 0)))
    conv = sum(conv_w[j] * up[:, j:j + L] for j in range(CONV_K))
    y_c = jax.nn.sigmoid(g_c) * (cb * conv)

    return (y_m.astype(h.dtype) + y_c) @ w_out

def hier_moe(h, w_group, b_group, w_router, b_router, w_gate, w_up, w_down):
    Bsz, L, D = h.shape
    f32 = jnp.float32
    t = h.reshape(-1, D)
    gl = (t @ w_group).astype(f32) + b_group.astype(f32)
    gp = jax.nn.softmax(gl, axis=-1)
    g_val, g_idx = lax.top_k(gp, 1)
    el = ((t @ w_router).astype(f32) + b_router.astype(f32)).reshape(-1, N_GROUPS, EXP_PER_GROUP)
    el_sel = jnp.take_along_axis(el, g_idx[:, :, None], axis=1)[:, 0]
    top_v, top_i = lax.top_k(el_sel, TOP_K)
    w = jax.nn.softmax(top_v, axis=-1) * g_val
    eid = g_idx * EXP_PER_GROUP + top_i
    gate = jnp.sum(jax.nn.one_hot(eid, N_EXPERTS, dtype=f32) * w[..., None], axis=1)
    hid = jax.nn.silu(jnp.einsum('nd,edf->nef', t, w_gate)) * jnp.einsum('nd,edf->nef', t, w_up)
    hid = hid * gate.astype(hid.dtype)[:, :, None]
    y = jnp.einsum('nef,efd->nd', hid, w_down)
    return y.reshape(Bsz, L, D)

def setup_inputs(seed: int = 0) -> dict:
    key = jax.random.key(seed)
    ks = jax.random.split(key, 18)

    def nrm(k, shape, scale):
        return jax.random.normal(k, shape, jnp.float32) * scale

    b_if = jnp.concatenate([nrm(ks[4], (DEPTH, M_HEADS), 0.1),
                            F_BIAS + nrm(ks[5], (DEPTH, M_HEADS), 0.5)], axis=-1)
    return {
        'x': nrm(ks[0], (BATCH, SEQ, D_MODEL), 1.0),
        'meta_tokens': nrm(ks[1], (N_META, D_MODEL), 1.0),
        'norm_mix': 1.0 + nrm(ks[2], (DEPTH, D_MODEL), 0.05),
        'w_in': nrm(ks[3], (DEPTH, D_MODEL, IN_TOTAL), D_MODEL ** -0.5),
        'b_if': b_if,
        'conv_w': nrm(ks[6], (DEPTH, CONV_K, CONV_WIDTH), CONV_K ** -0.5),
        'mh_gain': 1.0 + nrm(ks[7], (DEPTH, V_W), 0.05),
        'w_out': nrm(ks[8], (DEPTH, D_MODEL, D_MODEL), D_MODEL ** -0.5),
        'norm_ffn': 1.0 + nrm(ks[9], (DEPTH, D_MODEL), 0.05),
        'w_group': nrm(ks[10], (DEPTH, D_MODEL, N_GROUPS), D_MODEL ** -0.5),
        'b_group': nrm(ks[11], (DEPTH, N_GROUPS), 0.01),
        'w_router': nrm(ks[12], (DEPTH, D_MODEL, N_EXPERTS), D_MODEL ** -0.5),
        'b_router': nrm(ks[13], (DEPTH, N_EXPERTS), 0.01),
        'w_gate': nrm(ks[14], (DEPTH, N_EXPERTS, D_MODEL, D_EXPERT), D_MODEL ** -0.5),
        'w_up': nrm(ks[15], (DEPTH, N_EXPERTS, D_MODEL, D_EXPERT), D_MODEL ** -0.5),
        'w_down': nrm(ks[16], (DEPTH, N_EXPERTS, D_EXPERT, D_MODEL), D_EXPERT ** -0.5),
        'norm_final': 1.0 + nrm(ks[17], (D_MODEL,), 0.05),
    }

def reference(x, meta_tokens, norm_mix, w_in, b_if, conv_w, mh_gain, w_out, norm_ffn,
              w_group, b_group, w_router, b_router, w_gate, w_up, w_down, norm_final):
    Bsz = x.shape[0]
    meta = jnp.broadcast_to(meta_tokens[None], (Bsz, N_META, D_MODEL)).astype(x.dtype)
    h = jnp.concatenate([meta, x], axis=1)
    for l in range(DEPTH):
        h = h + hybrid_mixer(rmsnorm(h, norm_mix[l]), w_in[l], b_if[l], conv_w[l], mh_gain[l], w_out[l])
        h = h + hier_moe(rmsnorm(h, norm_ffn[l]), w_group[l], b_group[l], w_router[l], b_router[l],
                         w_gate[l], w_up[l], w_down[l])
    return rmsnorm(h, norm_final)[:, N_META:]


_drawn_inputs = setup_inputs


def setup_inputs(seed=0):
    import zlib

    import numpy as np

    out = dict(_drawn_inputs(seed))
    spreads = {}
    factors = {'b_router': 2.761}
    for name, (base, spread) in spreads.items():
        noise = np.random.default_rng([zlib.crc32(name.encode()), seed]).standard_normal(out[name].shape)
        drawn = base * np.exp(spread * noise) if base else spread * noise
        out[name] = jnp.asarray(drawn.astype(out[name].dtype))
    for name, factor in factors.items():
        out[name] = (out[name] * factor).astype(out[name].dtype)
    return out
```

```python
from contextlib import ExitStack

import concourse.bass as bass
from concourse import mybir

F32 = mybir.dt.float32
F16 = mybir.dt.float16
BF16 = mybir.dt.bfloat16
ALU = mybir.AluOpType
ACT = mybir.ActivationFunctionType
AX = mybir.AxisListType

P = 128
DEPTH = 2
D = 1024
KT = D // P
N_META = 16
SEQ = 256
T = N_META + SEQ
HEADS = 4
DV = D // HEADS
EPS = 1e-6
CONV_K = 3
N_GROUPS, PER_GROUP = 4, 4
EXPERTS = N_GROUPS * PER_GROUP
D_EXPERT = 256
FT = D_EXPERT // P
W_SCALE = 64.0
UNSCALE = 1.0 / W_SCALE
FAR = 1e30

TT = 3
TP = TT * P
T_START = [0, P, 2 * P]
T_SIZE = [P, P, T - 2 * P]
R_START = [0, P, T - P]
CAUSAL_AT = [0, T, T + (T - P)]
CAUSAL_W = [T, T - P, T - 2 * P]
CAUSAL = sum(CAUSAL_W)

Q, K, V0, GM0, CX0, CC0, CB0, GC0, PER_HEAD = 0, 1, 2, 4, 6, 8, 10, 12, 14
DENSE = HEADS * PER_HEAD + KT
RING = 7
PER_EXPERT = 3 * FT
MOE = EXPERTS * PER_EXPERT
M_RAW, M_SPLIT = PER_EXPERT, 2 * PER_EXPERT

C_MIX = 0
C_FFN = C_MIX + KT
C_GAIN = C_FFN + KT
C_CONV = C_GAIN + KT
C_GATE = C_CONV + CONV_K * KT
C_ROUTE = C_GATE + KT * 2 * HEADS
N_ROUTE = N_GROUPS + EXPERTS
C_BIF = C_ROUTE + KT * N_ROUTE
C_BROUTE = C_BIF + 1
C_ALL = C_BROUTE + N_ROUTE
F_ROW = 32
GROWS = F_ROW + HEADS

OPEN = 1


class Chain:

    def __init__(self, eng, sem, base, total):
        self.eng, self.sem, self.base, self.total, self.n = eng, sem, base, total, 0

    def step(self, ins):
        ins.then_inc(self.sem, 1)
        self.n += 1

    def settle(self):
        self.eng.wait_ge(self.sem, self.base + self.n)

    def end(self):
        assert self.n == self.total, (self.sem, self.n, self.total)


def ring_use(l, use, slot):
    return l * ((DENSE - slot + RING - 1) // RING) + use


def build(nc, h_in, params, norm_final, dense_w, moe_w, out):
    with ExitStack() as ctx:
        def sb(name, shape, dt=F32):
            return ctx.enter_context(nc.sbuf_tensor(name, shape, dt))

        def pb(name, shape, dt=F32):
            return ctx.enter_context(nc.psum_tensor(name, shape, dt))

        def sem(name):
            return ctx.enter_context(nc.semaphore(name))

        h_t = sb("h_t", [P, KT, T])
        norm_buf = sb("norm_buf", [P, KT, T])
        x_hi = sb("x_hi", [P, KT, T], F16)
        x_lo = sb("x_lo", [P, KT, T], F16)
        y_hi = sb("y_hi", [P, KT, T], F16)
        y_lo = sb("y_lo", [P, KT, T], F16)
        rstd = sb("rstd", [P, T])
        raw = sb("raw", [P, RING, D])
        w_hi = sb("w_hi", [P, RING, D], F16)
        w_lo = sb("w_lo", [P, RING, D], F16)
        m_raw = sb("m_raw", [P, M_RAW, D])
        m_hi = sb("m_hi", [P, M_SPLIT, D], F16)
        m_lo = sb("m_lo", [P, M_SPLIT, D], F16)
        prm_all = sb("prm_all", [P, DEPTH, C_ALL])
        prm = sb("prm", [P, C_ALL])
        fin_gain = sb("fin_gain", [P, KT])
        gate_hi = sb("gate_hi", [P, KT, GROWS], F16)
        gate_lo = sb("gate_lo", [P, KT, GROWS], F16)
        ones = sb("ones", [P, P])
        ident = sb("ident", [P, P])
        ident_b = sb("ident_b", [P, P], BF16)
        ahead = sb("ahead", [P, CAUSAL], BF16)
        eps = sb("eps", [P, 1])
        half = sb("half", [P, TT])
        one_row = sb("one_row", [GROWS, T])
        a_floor = sb("a_floor", [P, TP])
        a_col = sb("a_col", [P, TT, GROWS])
        scratch = sb("scratch", [P, HEADS * CAUSAL])
        cx, cv, ym = (scratch[:, i * 2 * T:(i + 1) * 2 * T].rearrange("p (a t) -> p a t", a=2) for i in range(3))
        g_pick = scratch[0:HEADS, :].rearrange("p (h c) -> p h c", h=HEADS)
        decay = norm_buf[:, :, :].rearrange("p k t -> p (k t)")[:, 0:HEADS * CAUSAL].rearrange("p (h c) -> p h c", h=HEADS)
        q_t = sb("q_t", [P, T])
        k_t = sb("k_t", [P, TP])
        v_t = sb("v_t", [P, 2, TP])
        v_n = sb("v_n", [P, TT, DV + 1])
        s_w = sb("s_w", [P, TT, TP])
        sig_m = sb("sig_m", [P, 2, T])
        sig_c = sb("sig_c", [P, 2, T])
        i_gate, f_sum, g_max, m_row = (b[0:HEADS, j, :] for b in (sig_m, sig_c) for j in range(2))
        f_gate, f_abs, f_exp, f_log = (b[F_ROW:GROWS, j, :] for b in (sig_m, sig_c) for j in range(2))
        u = sb("u", [P, 2, T + CONV_K - 1])
        hm = sb("hm", [P, TT, DV])
        ssq = sb("ssq", [P, TT])
        den = sb("den", [P, TT])
        stat = sb("stat", [P, 6, TT])
        lg = sb("lg", [P, TT, N_ROUTE])
        rt = sb("rt", [P, 12, TT, EXPERTS])
        small = sb("small", [P, 24, TT])
        iota_e = sb("iota_e", [P, TT, 4])
        gate_n = sb("gate_n", [P, TT, EXPERTS])
        gate_t, gate_pick = cv[0:EXPERTS, 0, :], cv[0:EXPERTS, 1, :]
        gate_b, sg, hid = q_t, sig_m, sig_c
        hid_hi = sb("hid_hi", [P, FT, T], F16)
        hid_lo = sb("hid_lo", [P, FT, T], F16)

        acc = [pb(f"acc{i}", [P, 512]) for i in range(2)]
        b_s = pb("b_s", [P, 512])
        b_t = pb("b_t", [P, 512])
        num = pb("num", [P, TT, 512])
        misc = pb("misc", [P, 512])

        h_loaded = sem("h_loaded")
        prm_loaded = sem("prm_loaded")
        consts = sem("consts")
        zeroed = sem("zeroed")
        padded = sem("padded")
        raw_landed = [sem(f"raw_landed{i}") for i in range(RING)]
        hi_done = sem("hi_done")
        lo_done = sem("lo_done")
        tiles_done = sem("tiles_done")
        m_landed = [sem(f"m_landed{i}") for i in range(M_RAW)]
        m_hi_done = sem("m_hi_done")
        m_lo_done = sem("m_lo_done")
        down_done = sem("down_done")
        prep_done = sem("prep_done")
        sq_ready = sem("sq_ready")
        ms_ready = sem("ms_ready")
        std_ready = sem("std_ready")
        rstd_ready = sem("rstd_ready")
        x_ready = sem("x_ready")
        x_hi_ready = sem("x_hi_ready")
        x_lo_ready = sem("x_lo_ready")
        gates_ready = sem("gates_ready")
        gate_step = sem("gate_step")
        f_abs_ready = sem("f_abs_ready")
        f_exp_ready = sem("f_exp_ready")
        f_log_ready = sem("f_log_ready")
        m_row_ready = sem("m_row_ready")
        floor_ready = sem("floor_ready")
        a_ready = sem("a_ready")
        pick_ready = sem("pick_ready")
        a_col_ps = sem("a_col_ps")
        a_col_ready = sem("a_col_ready")
        arg_ready = sem("arg_ready")
        decay_ready = sem("decay_ready")
        qkv_ready = sem("qkv_ready")
        v_turned = sem("v_turned")
        v_n_ready = sem("v_n_ready")
        scores_ready = sem("scores_ready")
        s_w_ready = sem("s_w_ready")
        num_ready = sem("num_ready")
        ssq_ready = sem("ssq_ready")
        head_step = sem("head_step")
        var_ready = sem("var_ready")
        pow_ready = sem("pow_ready")
        f_ready = sem("f_ready")
        hm_ready = sem("hm_ready")
        hm_turned = sem("hm_turned")
        sig_m_ready = sem("sig_m_ready")
        sig_c_ready = sem("sig_c_ready")
        cx_ready = sem("cx_ready")
        y_ready = sem("y_ready")
        ym_ready = sem("ym_ready")
        cc_read = sem("cc_read")
        cb_read = sem("cb_read")
        h_mixed = sem("h_mixed")
        logits_ready = sem("logits_ready")
        route_step = sem("route_step")
        exp_in_ready = sem("exp_in_ready")
        exp_ready = sem("exp_ready")
        gate_n_ready = sem("gate_n_ready")
        gate_t_ps = sem("gate_t_ps")
        gate_t_ready = sem("gate_t_ready")
        gate_pick_ready = sem("gate_pick_ready")
        gate_b_ps = sem("gate_b_ps")
        gu_ready = sem("gu_ready")
        sg_ready = sem("sg_ready")
        silu_ready = sem("silu_ready")
        gate_b_ready = sem("gate_b_ready")
        hid_mid = sem("hid_mid")
        hid_hi_ready = sem("hid_hi_ready")
        hid_ready = sem("hid_ready")
        hid_lo_ready = sem("hid_lo_ready")
        down_added = sem("down_added")
        out_stored = sem("out_stored")

        block = ctx.enter_context(nc.Block())

        N_CONST = 8

        @block.sync
        def _(sp):
            sp.dma_start(h_t[:, :, :], h_in).then_inc(h_loaded, 16)
            sp.dma_start(prm_all[:, :, :], params).then_inc(prm_loaded, 16)
            sp.dma_start(fin_gain[:, :], norm_final).then_inc(prm_loaded, 16)

            def load_dense(l, n, slot):
                sp.wait_ge(lo_done, l * DENSE + n + 1)
                sp.dma_start(raw[:, slot, :], dense_w[l, n]).then_inc(raw_landed[slot], 16)

            with sp.Fori(0, DEPTH) as l:
                with sp.Fori(0, HEADS) as h:
                    for i in range(PER_HEAD):
                        load_dense(l, h * PER_HEAD + i, i % RING)
                for m in range(KT):
                    n = HEADS * PER_HEAD + m
                    load_dense(l, n, n % RING)
                with sp.Fori(0, EXPERTS) as e:
                    for i in range(PER_EXPERT):
                        sp.wait_ge(m_lo_done, l * MOE + e * PER_EXPERT + i + 1)
                        sp.dma_start(m_raw[:, i, :], moe_w[l, e * PER_EXPERT + i]).then_inc(m_landed[i], 16)
            for k in range(KT):
                sp.wait_ge(x_ready, 2 * DEPTH * KT + k + 1)
                sp.dma_start(out[:, k, :], norm_buf[:, k, N_META:]).then_inc(out_stored, 16)
            sp.wait_ge(out_stored, 16 * KT)

        @block.gpsimd
        def _(pool):
            pool.memset(ones[:, :], 1.0).then_inc(consts, 1)
            pool.memset(ident[:, :], 0.0).then_inc(zeroed, 1)
            pool.memset(ahead[:, :], 0.0).then_inc(zeroed, 1)
            pool.wait_ge(zeroed, 2)
            pool.affine_select(out=ident[:, :], in_=ident[:, :], compare_op=ALU.not_equal, fill=1.0,
                               base=0, pattern=[[-1, P]], channel_multiplier=1).then_inc(consts, 1)
            pool.wait_ge(consts, 2)
            pool.tensor_copy(ident_b[:, :], ident[:, :]).then_inc(consts, 1)
            for at, w in zip(CAUSAL_AT, CAUSAL_W):
                pool.affine_select(out=ahead[:, at:at + w], in_=ahead[:, at:at + w], compare_op=ALU.is_ge,
                                   fill=FAR, base=0, pattern=[[1, w]], channel_multiplier=-1).then_inc(consts, 1)
            pool.memset(eps[:, :], EPS).then_inc(consts, 1)
            pool.memset(half[:, :], -0.5).then_inc(consts, 1)
            with pool.Fori(0, DEPTH) as l:
                with pool.Fori(0, HEADS) as h:
                    hd = l * HEADS + h
                    pool.wait_ge(var_ready, hd + 1)
                    pool.tensor_tensor(stat[:, 4, :], stat[:, 3, :], half[:, :], ALU.pow).then_inc(pow_ready, 1)

        @block.scalar
        def _(act):
            def hi_dense(l, n, slot, use):
                act.wait_ge(raw_landed[slot], (ring_use(l, use, slot) + 1) * 16)
                act.wait_ge(tiles_done, l * DENSE + n + 1)
                act.activation(w_hi[:, slot, :], raw[:, slot, :], ACT.Copy, scale=W_SCALE).then_inc(hi_done, 1)

            def norm(i):
                for k in range(KT):
                    act.activation(norm_buf[:, k, :], h_t[:, k, :], ACT.Square).then_inc(sq_ready, 1)
                act.wait_ge(ms_ready, i + 1)
                act.activation(rstd[:, :], misc[:, 0:T], ACT.Sqrt, bias=eps[:, 0:1], scale=1.0 / D)\
                   .then_inc(std_ready, 1)

            def norm_hi(i):
                for k in range(KT):
                    act.wait_ge(x_ready, i * KT + k + 1)
                    act.activation(x_hi[:, k, :], norm_buf[:, k, :], ACT.Copy).then_inc(x_hi_ready, 1)

            act.wait_ge(h_loaded, 16)
            act.wait_ge(consts, N_CONST)
            with act.Fori(0, DEPTH) as l:
                for n in range(3):
                    hi_dense(l, n, n, 0)
                act.wait_ge(down_added, OPEN + l * EXPERTS * KT)
                norm(l * 2)
                norm_hi(l * 2)
                act.wait_ge(f_abs_ready, l + 1)
                act.activation(f_exp, f_abs, ACT.Exp, scale=-1.0)\
                   .then_inc(f_exp_ready, 1)
                act.wait_ge(f_exp_ready, l + 1)
                act.activation(f_log, f_exp, ACT.Ln, bias=1.0)\
                   .then_inc(f_log_ready, 1)
                act.wait_ge(m_row_ready, l + 1)
                act.activation(a_floor[F_ROW:GROWS, 0:T], m_row, ACT.Exp, scale=-1.0)\
                   .then_inc(floor_ready, 1)
                act.wait_ge(a_col_ready, l + 1)
                for h in range(HEADS):
                    act.wait_ge(arg_ready, l * HEADS + h + 1)
                    for s in range(TT):
                        at, w, sz = CAUSAL_AT[s], CAUSAL_W[s], P
                        act.activation(decay[:, h, at:at + w], [b_s, b_t][h % 2][:, at:at + w], ACT.Exp,
                                       bias=a_col[:, s, h:h + 1], scale=-1.0).then_inc(decay_ready, 1)

                with act.Fori(0, HEADS) as h:
                    hd = l * HEADS + h
                    tile0 = l * DENSE + h * PER_HEAD
                    for i in range(PER_HEAD):
                        nxt = i + 3
                        hi_dense(l, h * PER_HEAD + nxt, nxt % RING, h * 2 + nxt // RING)
                        if i == V0 + 3:
                            act.wait_ge(v_turned, hd + 1)
                            act.activation(v_n[:, :, 0:DV], num[:, :, 0:DV], ACT.Copy).then_inc(v_n_ready, 1)
                        if i == CC0:
                            act.wait_ge(num_ready, hd + 1)
                            for t in range(TT):
                                act.activation(hm[:, t, :], num[:, t, 0:DV], ACT.Square,
                                               accum_out=ssq[:, t:t + 1]).then_inc(ssq_ready, 1)
                            act.activation(den[:, :], num[:, :, DV], ACT.Copy).then_inc(ssq_ready, 1)
                        if i == CC0 + 1:
                            act.wait_ge(f_ready, hd + 1)
                            for t in range(TT):
                                act.activation(hm[:, t, :], num[:, t, 0:DV], ACT.Copy,
                                               scale=stat[:, 5, t:t + 1]).then_inc(hm_ready, 1)
                        if i in (GM0, GM0 + 1, CX0, CX0 + 1, GC0, GC0 + 1):
                            act.wait_ge(tiles_done, RING + tile0 + i + 1)
                            if i == GM0:
                                act.wait_ge(ym_ready, OPEN + hd * 2)
                            if i == GC0:
                                act.wait_ge(y_ready, OPEN + hd)
                            dst, func, ready = {GM0: (sig_m, ACT.Sigmoid, sig_m_ready), CX0: (cx, ACT.Copy, cx_ready),
                                                GC0: (sig_c, ACT.Sigmoid, sig_c_ready)}[i - i % 2]
                            act.activation(dst[:, i % 2, :], acc[i % 2][:, 0:T], func, scale=UNSCALE)\
                               .then_inc(ready, 1)
                for m in range(KT):
                    if m + 3 < KT:
                        n = HEADS * PER_HEAD + m + 3
                        hi_dense(l, n, n % RING, n // RING)

                act.wait_ge(h_mixed, (l + 1) * KT)
                norm(l * 2 + 1)
                norm_hi(l * 2 + 1)
                act.wait_ge(exp_in_ready, l + 1)
                act.activation(small[:, 8:13, :], small[:, 0:5, :], ACT.Exp).then_inc(exp_ready, 1)
                with act.Fori(0, EXPERTS // 2) as pair:
                    for s in range(2):
                        ex = l * EXPERTS + pair * 2 + s
                        act.wait_ge(down_done, OPEN + ex * KT)
                        for i in range(PER_EXPERT):
                            act.wait_ge(m_landed[i], (ex + 1) * 16)
                            act.activation(m_hi[:, s * PER_EXPERT + i, :], m_raw[:, i, :], ACT.Copy, scale=W_SCALE)\
                               .then_inc(m_hi_done, 1)
                        for f in range(FT):
                            act.wait_ge(gu_ready, ex * 2 * FT + f + 1)
                            act.wait_ge(hid_mid, OPEN + ex * FT)
                            act.activation(sg[:, f, :], acc[f][:, 0:T], ACT.Sigmoid, scale=UNSCALE)\
                               .then_inc(sg_ready, 1)
                        for f in range(FT):
                            act.wait_ge(hid_ready, ex * FT + f + 1)
                            act.wait_ge(down_done, OPEN + KT + ex * KT)
                            act.activation(hid_hi[:, f, :], hid[:, f, :], ACT.Copy).then_inc(hid_hi_ready, 1)
            act.wait_ge(down_added, OPEN + DEPTH * EXPERTS * KT)
            norm(2 * DEPTH)

        PREP, GATE, HEAD, ROUTE = 5, 9, 14, 32

        @block.vector
        def _(dve):
            init = Chain(dve, padded, 0, 9)
            init.step(dve.memset(k_t[:, :], 0.0))
            init.step(dve.memset(v_t[:, :, :], 0.0))
            init.step(dve.memset(s_w[:, :, :], 0.0))
            init.step(dve.memset(v_n[:, :, DV:DV + 1], 1.0))
            init.step(dve.memset(u[:, :, 0:CONV_K - 1], 0.0))
            init.step(dve.memset(a_floor[:, :], 1.0))
            init.step(dve.memset(one_row[:, :], 1.0))
            init.step(dve.memset(gate_hi[:, :, :], 0.0))
            init.step(dve.memset(gate_lo[:, :, :], 0.0))
            init.end()
            dve.memset(rstd[0:1, 0:1], 0.0).then_inc(lo_done, RING)
            dve.memset(rstd[0:1, 1:2], 0.0).then_inc(tiles_done, RING)
            dve.memset(rstd[0:1, 2:3], 0.0).then_inc(m_lo_done, M_RAW)
            dve.memset(rstd[0:1, 3:4], 0.0).then_inc(down_done, OPEN + KT)
            for n, s in enumerate((ym_ready, sig_c_ready, hm_ready, y_ready, down_added, silu_ready, hid_mid,
                                   gate_b_ready)):
                dve.memset(rstd[0:1, 4 + n:5 + n], 0.0).then_inc(s, OPEN)
            for e in range(4):
                dve.memset(iota_e[:, :, e:e + 1], float(e)).then_inc(padded, 1)
            dve.wait_ge(padded, 9 + 4)
            dve.wait_ge(prm_loaded, 32)
            dve.wait_ge(consts, N_CONST)
            dve.wait_ge(h_loaded, 16)

            def lo_dense(l, n, slot):
                dve.wait_ge(hi_done, l * DENSE + n + 1)
                dve.scalar_tensor_tensor(w_lo[:, slot, :], raw[:, slot, :], W_SCALE, w_hi[:, slot, :],
                                         ALU.mult, ALU.subtract).then_inc(lo_done, 1)

            def norm(i, gain, split=True):
                dve.wait_ge(std_ready, i + 1)
                dve.reciprocal(rstd[:, :], rstd[:, :]).then_inc(rstd_ready, 1)
                dve.wait_ge(rstd_ready, i + 1)

                def low(k):
                    dve.wait_ge(x_hi_ready, i * KT + k + 1)
                    dve.tensor_tensor(x_lo[:, k, :], norm_buf[:, k, :], x_hi[:, k, :], ALU.subtract)\
                       .then_inc(x_lo_ready, 1)
                for k in range(KT):
                    dve.scalar_tensor_tensor(norm_buf[:, k, :], h_t[:, k, :], gain[:, k:k + 1], rstd[:, :],
                                             ALU.mult, ALU.mult).then_inc(x_ready, 1)
                    if split and k:
                        low(k - 1)
                if split:
                    low(KT - 1)

            with dve.Fori(0, DEPTH) as l:
                prep = Chain(dve, prep_done, l * PREP, PREP)
                prep.step(dve.tensor_scalar(prm[:, :], prm_all[:, l, :], 1.0, None, ALU.mult))
                prep.settle()
                gw = prm[:, C_GATE:C_ROUTE].rearrange("p (k g) -> p k g", k=KT)
                for g, row in ((0, 0), (HEADS, F_ROW)):
                    prep.step(dve.tensor_scalar(gate_hi[:, :, row:row + HEADS], gw[:, :, g:g + HEADS], W_SCALE, None,
                                                ALU.mult))
                prep.settle()
                for g, row in ((0, 0), (HEADS, F_ROW)):
                    prep.step(dve.scalar_tensor_tensor(gate_lo[:, :, row:row + HEADS], gw[:, :, g:g + HEADS], W_SCALE,
                                                       gate_hi[:, :, row:row + HEADS], ALU.mult, ALU.subtract))
                prep.end()
                lo_dense(l, 0, 0)
                lo_dense(l, 1, 1)
                norm(l * 2, prm[:, C_MIX:C_MIX + KT])

                dve.wait_ge(gates_ready, l + 1)
                g = Chain(dve, gate_step, l * GATE, GATE)
                g.step(dve.tensor_scalar(i_gate, misc[0:HEADS, 0:T], UNSCALE, prm[0:HEADS, C_BIF:C_BIF + 1],
                                         ALU.mult, ALU.add))
                g.step(dve.tensor_scalar(f_gate, misc[F_ROW:GROWS, 0:T], UNSCALE,
                                         prm[F_ROW:GROWS, C_BIF:C_BIF + 1], ALU.mult, ALU.add))
                g.settle()
                dve.scalar_tensor_tensor(f_abs, f_gate, -1.0, f_gate, ALU.mult, ALU.max)\
                   .then_inc(f_abs_ready, 1)
                dve.wait_ge(f_log_ready, l + 1)
                g.step(dve.scalar_tensor_tensor(f_log, f_gate, 0.0,
                                                f_log, ALU.min, ALU.subtract))
                g.settle()
                g.step(dve.tensor_tensor_scan(f_sum, one_row[F_ROW:GROWS, :], f_log, 0.0,
                                              ALU.mult, ALU.add))
                g.settle()
                g.step(dve.tensor_tensor(a_floor[0:HEADS, 0:T], i_gate, f_sum, ALU.subtract))
                g.settle()
                g.step(dve.tensor_tensor_scan(g_max, a_floor[0:HEADS, 0:T], a_floor[0:HEADS, 0:T], 0.0,
                                              ALU.max, ALU.max))
                g.settle()
                dve.tensor_tensor(m_row, f_sum, g_max, ALU.add).then_inc(m_row_ready, 1)
                for s in range(TT):
                    at, w = CAUSAL_AT[s], CAUSAL_W[s]
                    g.step(dve.tensor_copy(g_pick[:, 0, at:at + w], g_max[:, T_START[s]:T]))
                g.settle()
                for h in reversed(range(HEADS)):
                    dve.tensor_scalar(g_pick[:, h, :], g_pick[:, 0, :], ident[0:HEADS, h:h + 1], None, ALU.mult)\
                       .then_inc(pick_ready, 1)
                g.end()
                dve.wait_ge(a_col_ps, l + 1)
                dve.tensor_copy(a_col[:, :, :], misc[:, 0:TP].rearrange("p (t g) -> p t g", t=TT)[:, :, 0:GROWS])\
                   .then_inc(a_col_ready, 1)

                with dve.Fori(0, HEADS) as h:
                    hd = l * HEADS + h
                    tile0 = l * DENSE + h * PER_HEAD
                    c = Chain(dve, head_step, hd * HEAD, HEAD)
                    for i in range(PER_HEAD):
                        nxt = i + 2
                        lo_dense(l, h * PER_HEAD + nxt, nxt % RING)
                        b, ct = acc[i % 2][:, 0:T], i % 2
                        if i in (Q, K, V0, V0 + 1, CC0, CC0 + 1, CB0, CB0 + 1):
                            dve.wait_ge(tiles_done, RING + tile0 + i + 1)
                        if i in (Q, K, V0, V0 + 1):
                            dst = {Q: q_t[:, :], K: k_t[:, 0:T], V0: v_t[:, 0, 0:T], V0 + 1: v_t[:, 1, 0:T]}[i]
                            dve.tensor_scalar(dst, b, UNSCALE, None, ALU.mult).then_inc(qkv_ready, 1)
                        if i == GM0 + 1:
                            dve.wait_ge(scores_ready, hd + 1)
                            dve.wait_ge(decay_ready, (l + 1) * HEADS * TT)
                            for s in range(TT):
                                at, w = CAUSAL_AT[s], CAUSAL_W[s]
                                dve.scalar_tensor_tensor(s_w[:, s, T_START[s]:T], b_s[:, at:at + w], P ** -0.5,
                                                         decay[:, h, at:at + w], ALU.mult, ALU.mult)\
                                   .then_inc(s_w_ready, 1)
                        if i in (CC0, CC0 + 1):
                            dve.wait_ge(cx_ready, hd * 2 + ct + 1)
                            dve.scalar_tensor_tensor(u[:, ct, CONV_K - 1:], b, UNSCALE, cx[:, ct, :],
                                                     ALU.mult, ALU.mult).then_inc(cc_read, 1)
                            dve.wait_ge(cc_read, hd * 2 + ct + 1)
                            tap = [prm[:, C_CONV + j * KT:C_CONV + (j + 1) * KT] for j in range(CONV_K)]
                            c.step(dve.tensor_scalar(cv[:, ct, :], u[:, ct, 0:T], tap[0][:, bass.ds(h * 2 + ct, 1)],
                                                     None, ALU.mult))
                            for j in range(1, CONV_K):
                                c.settle()
                                c.step(dve.scalar_tensor_tensor(cv[:, ct, :], u[:, ct, j:j + T],
                                                                tap[j][:, bass.ds(h * 2 + ct, 1)], cv[:, ct, :],
                                                                ALU.mult, ALU.add))
                        if i == CC0:
                            dve.wait_ge(ssq_ready, (hd + 1) * (TT + 1))
                            c.step(dve.scalar_tensor_tensor(stat[:, 0, :], den[:, :], -1.0, den[:, :],
                                                            ALU.mult, ALU.max))
                            c.settle()
                            dve.wait_ge(a_col_ready, l + 1)
                            c.step(dve.tensor_tensor(stat[:, 0, :], stat[:, 0, :],
                                                     a_col[:, :, bass.ds(F_ROW + h, 1)].rearrange("p t o -> p (t o)"),
                                                     ALU.max))
                            c.settle()
                            c.step(dve.reciprocal(stat[:, 1, :], stat[:, 0, :]))
                            c.settle()
                            c.step(dve.tensor_tensor(stat[:, 2, :], ssq[:, :], stat[:, 1, :], ALU.mult))
                            c.settle()
                            c.step(dve.tensor_tensor(stat[:, 2, :], stat[:, 2, :], stat[:, 1, :], ALU.mult))
                            c.settle()
                            dve.tensor_scalar(stat[:, 3, :], stat[:, 2, :], 1.0 / DV, EPS, ALU.mult, ALU.add)\
                               .then_inc(var_ready, 1)
                            dve.wait_ge(pow_ready, hd + 1)
                            dve.tensor_tensor(stat[:, 5, :], stat[:, 1, :], stat[:, 4, :], ALU.mult)\
                               .then_inc(f_ready, 1)
                        if i in (CB0, CB0 + 1):
                            c.settle()
                            dve.scalar_tensor_tensor(cv[:, ct, :], b, UNSCALE, cv[:, ct, :],
                                                     ALU.mult, ALU.mult).then_inc(cb_read, 1)
                        if i == GC0:
                            dve.wait_ge(hm_turned, hd + 1)
                            dve.wait_ge(sig_m_ready, (hd + 1) * 2)
                            for v, bank in enumerate((b_s, b_t)):
                                dve.scalar_tensor_tensor(ym[:, v, :], bank[:, 0:T],
                                                         prm[:, bass.ds(C_GAIN + h * 2 + v, 1)],
                                                         sig_m[:, v, :], ALU.mult, ALU.mult).then_inc(ym_ready, 1)
                    dve.wait_ge(sig_c_ready, OPEN + (hd + 1) * 2)
                    dve.wait_ge(cb_read, (hd + 1) * 2)
                    c.step(dve.tensor_tensor(cv[:, :, :], cv[:, :, :], sig_c[:, :, :], ALU.mult))
                    c.settle()
                    dve.wait_ge(ym_ready, OPEN + (hd + 1) * 2)
                    c.step(dve.tensor_tensor(ym[:, :, :], cv[:, :, :], ym[:, :, :], ALU.add))
                    c.settle()
                    c.step(dve.tensor_scalar(y_hi[:, bass.ds(h * 2, 2), :], ym[:, :, :], 1.0, None, ALU.mult))
                    c.settle()
                    dve.tensor_tensor(y_lo[:, bass.ds(h * 2, 2), :], ym[:, :, :], y_hi[:, bass.ds(h * 2, 2), :],
                                      ALU.subtract).then_inc(y_ready, 1)
                    c.end()

                for m in range(KT):
                    n = HEADS * PER_HEAD + m
                    if m + 2 < KT:
                        lo_dense(l, n + 2, (n + 2) % RING)
                    dve.wait_ge(tiles_done, RING + l * DENSE + n + 1)
                    dve.scalar_tensor_tensor(h_t[:, m, :], acc[n % 2][:, 0:T], UNSCALE, h_t[:, m, :],
                                             ALU.mult, ALU.add).then_inc(h_mixed, 1)

                dve.wait_ge(h_mixed, (l + 1) * KT)
                norm(l * 2 + 1, prm[:, C_FFN:C_FFN + KT])

                r = Chain(dve, route_step, l * ROUTE, ROUTE)

                def then(ins):
                    r.step(ins)
                    r.settle()

                dve.wait_ge(logits_ready, l + 1)
                then(dve.tensor_copy(lg[:, :, :], misc[:, 0:TT * N_ROUTE].rearrange("p (t g) -> p t g", t=TT)))
                gl = lg[:, :, 0:N_GROUPS]
                el = lg[:, :, N_GROUPS:]

                def quad(i):
                    return rt[:, i, :, 0:4]

                def col(i):
                    return small[:, i, :]

                def first_max(values, best, pick, tmp, idx):
                    then(dve.tensor_reduce(col(best), values, AX.X, ALU.max))
                    then(dve.tensor_tensor(tmp, values, col(best).unsqueeze(2).broadcast_to([P, TT, 4]), ALU.is_equal))
                    then(dve.scalar_tensor_tensor(tmp, tmp, -8.0, iota_e[:, :, :], ALU.mult, ALU.add))
                    then(dve.tensor_reduce(col(idx), tmp, AX.X, ALU.min))
                    then(dve.tensor_scalar(col(idx), col(idx), 8.0, None, ALU.add))
                    then(dve.tensor_tensor(pick, iota_e[:, :, :], col(idx).unsqueeze(2).broadcast_to([P, TT, 4]),
                                           ALU.is_equal))

                first_max(gl, 14, quad(0), quad(1), 15)
                ex_in = small[:, 0:4, :].rearrange("p g t -> p t g")
                then(dve.tensor_tensor(ex_in, gl, col(14).unsqueeze(2).broadcast_to([P, TT, 4]), ALU.subtract))
                chosen = rt[:, 2, :, :].rearrange("p t (g e) -> p t g e", g=N_GROUPS)
                then(dve.tensor_tensor(chosen, el.rearrange("p t (g e) -> p t g e", g=N_GROUPS),
                                       quad(0).unsqueeze(3).broadcast_to([P, TT, N_GROUPS, PER_GROUP]), ALU.mult))
                then(dve.tensor_reduce(quad(3), chosen.rearrange("p t g e -> p t e g"), AX.X, ALU.add))
                first_max(quad(3), 16, quad(4), quad(5), 17)
                then(dve.scalar_tensor_tensor(quad(6), quad(4), -FAR, quad(3), ALU.mult, ALU.add))
                first_max(quad(6), 18, quad(7), quad(5), 19)
                dve.tensor_tensor(col(4), col(18), col(16), ALU.subtract).then_inc(exp_in_ready, 1)
                dve.wait_ge(exp_ready, l + 1)
                then(dve.tensor_reduce(col(20), small[:, 8:12, :].rearrange("p g t -> p t g"), AX.X, ALU.add))
                then(dve.tensor_scalar(col(21), col(12), 1.0, None, ALU.add))
                then(dve.tensor_tensor(col(20), col(20), col(21), ALU.mult))
                then(dve.reciprocal(col(22), col(20)))
                then(dve.tensor_tensor(col(23), col(22), col(12), ALU.mult))
                then(dve.tensor_tensor(quad(8), quad(4), col(22).unsqueeze(2).broadcast_to([P, TT, 4]), ALU.mult))
                then(dve.tensor_tensor(quad(9), quad(7), col(23).unsqueeze(2).broadcast_to([P, TT, 4]), ALU.mult))
                then(dve.tensor_tensor(quad(8), quad(8), quad(9), ALU.add))
                then(dve.tensor_copy(rt[:, 10, :, :].rearrange("p t (g e) -> p t g e", g=N_GROUPS),
                                     quad(0).unsqueeze(3).broadcast_to([P, TT, N_GROUPS, PER_GROUP])))
                dve.tensor_tensor(gate_n[:, :, :].rearrange("p t (g e) -> p t g e", g=N_GROUPS),
                                  rt[:, 10, :, :].rearrange("p t (g e) -> p t g e", g=N_GROUPS),
                                  quad(8).unsqueeze(2).broadcast_to([P, TT, N_GROUPS, PER_GROUP]), ALU.mult)\
                   .then_inc(gate_n_ready, 1)
                r.end()
                dve.wait_ge(gate_t_ps, l + 1)
                dve.tensor_copy(gate_t, misc[0:EXPERTS, 0:T]).then_inc(gate_t_ready, 1)

                with dve.Fori(0, EXPERTS // 2) as pair:
                    for s in range(2):
                        ex = l * EXPERTS + pair * 2 + s
                        for i in range(PER_EXPERT):
                            slot = s * PER_EXPERT + i
                            dve.wait_ge(m_hi_done, ex * PER_EXPERT + i + 1)
                            dve.scalar_tensor_tensor(m_lo[:, slot, :], m_raw[:, i, :], W_SCALE, m_hi[:, slot, :],
                                                     ALU.mult, ALU.subtract).then_inc(m_lo_done, 1)
                        dve.wait_ge(gate_t_ready, l + 1)
                        dve.tensor_scalar(gate_pick, gate_t, ident[0:EXPERTS, bass.ds(pair * 2 + s, 1)],
                                          None, ALU.mult).then_inc(gate_pick_ready, 1)
                        dve.wait_ge(gate_b_ps, ex + 1)
                        dve.tensor_copy(gate_b[:, :], misc[:, 0:T]).then_inc(gate_b_ready, 1)
                        for f in range(FT):
                            dve.wait_ge(sg_ready, ex * FT + f + 1)
                            dve.scalar_tensor_tensor(sg[:, f, :], acc[f][:, 0:T], UNSCALE, sg[:, f, :],
                                                     ALU.mult, ALU.mult).then_inc(silu_ready, 1)
                            dve.wait_ge(silu_ready, OPEN + ex * FT + f + 1)
                            dve.wait_ge(gu_ready, ex * 2 * FT + FT + f + 1)
                            dve.scalar_tensor_tensor(hid[:, f, :], [b_s, b_t][f][:, 0:T], UNSCALE, sg[:, f, :],
                                                     ALU.mult, ALU.mult).then_inc(hid_mid, 1)
                            dve.wait_ge(hid_mid, OPEN + ex * FT + f + 1)
                            dve.wait_ge(gate_b_ready, OPEN + ex + 1)
                            dve.tensor_tensor(hid[:, f, :], hid[:, f, :], gate_b[:, :], ALU.mult)\
                               .then_inc(hid_ready, 1)
                            dve.wait_ge(hid_hi_ready, ex * FT + f + 1)
                            dve.tensor_tensor(hid_lo[:, f, :], hid[:, f, :], hid_hi[:, f, :], ALU.subtract)\
                               .then_inc(hid_lo_ready, 1)
                        for m in range(KT):
                            dve.wait_ge(down_done, OPEN + KT + ex * KT + m + 1)
                            dve.scalar_tensor_tensor(h_t[:, m, :], num[:, m % TT, 0:T], UNSCALE, h_t[:, m, :],
                                                     ALU.mult, ALU.add).then_inc(down_added, 1)
                        dve.wait_ge(down_added, OPEN + (ex + 1) * KT)
            norm(2 * DEPTH, fin_gain, split=False)

        @block.tensor
        def _(pe):
            pe.wait_ge(consts, N_CONST)
            pe.wait_ge(padded, 9 + 4)

            def mean_square(i):
                for k in range(KT):
                    pe.wait_ge(sq_ready, i * KT + k + 1)
                    mm = pe.matmul(misc[:, 0:T], ones[:, :], norm_buf[:, k, :], start=(k == 0), stop=(k == KT - 1))
                mm.then_inc(ms_ready, 1)

            def three(dst, hi, lo, rhi, rlo, first, last):
                pe.matmul(dst, hi, rhi, start=first, stop=False)
                pe.matmul(dst, hi, rlo, start=False, stop=False)
                return pe.matmul(dst, lo, rhi, start=False, stop=last)

            def dense(l, n, slot, bank, rhi, rlo):
                pe.wait_ge(lo_done, RING + l * DENSE + n + 1)
                for k in range(KT):
                    cols = slice(k * P, (k + 1) * P)
                    mm = three(acc[bank][:, 0:T], w_hi[:, slot, cols], w_lo[:, slot, cols], rhi[:, k, :], rlo[:, k, :],
                               k == 0, k == KT - 1)
                mm.then_inc(tiles_done, 1)

            with pe.Fori(0, DEPTH) as l:
                mean_square(l * 2)
                pe.wait_ge(prep_done, (l + 1) * PREP)
                pe.wait_ge(std_ready, l * 2 + 1)
                for k in range(KT):
                    pe.wait_ge(x_lo_ready, l * 2 * KT + k + 1)
                    mm = three(misc[0:GROWS, 0:T], gate_hi[:, k, :], gate_lo[:, k, :], x_hi[:, k, :], x_lo[:, k, :],
                               k == 0, k == KT - 1)
                mm.then_inc(gates_ready, 1)
                pe.wait_ge(floor_ready, l + 1)
                for t in range(TT):
                    mm = pe.transpose(misc[:, t * P:(t + 1) * P], a_floor[:, t * P:(t + 1) * P], ident[:, :])
                mm.then_inc(a_col_ps, 1)
                for h in range(HEADS):
                    bank = [b_s, b_t][h % 2]
                    pe.wait_ge(pick_ready, (l + 1) * HEADS)
                    if h >= 2:
                        pe.wait_ge(decay_ready, (l * HEADS + h - 1) * TT)
                    pe.matmul(bank[:, 0:CAUSAL], ones[0:HEADS, :], g_pick[:, h, :], start=True, stop=False)
                    pe.matmul(bank[:, 0:CAUSAL], ident_b[:, :], ahead[:, :], start=False, stop=True)\
                      .then_inc(arg_ready, 1)
                with pe.Fori(0, HEADS) as h:
                    hd = l * HEADS + h
                    for i in range(PER_HEAD):
                        prev = (i - 2) % PER_HEAD
                        if i < 2:
                            pe.wait_ge(sig_c_ready, OPEN + hd * 2)
                        elif prev < GM0:
                            pe.wait_ge(qkv_ready, hd * 4 + prev + 1)
                        else:
                            read = {GM0: sig_m_ready, CX0: cx_ready, CC0: cc_read, CB0: cb_read}[prev - prev % 2]
                            pe.wait_ge(read, hd * 2 + prev % 2 + 1)
                        dense(l, h * PER_HEAD + i, i % RING, i % 2, x_hi, x_lo)
                        if i == GM0:
                            pe.wait_ge(qkv_ready, hd * 4 + 4)
                            pe.wait_ge(hm_ready, OPEN + hd * TT)
                            for t in range(TT):
                                for v in range(2):
                                    mm = pe.transpose(num[:, t, v * P:(v + 1) * P], v_t[:, v, t * P:(t + 1) * P],
                                                      ident[:, :])
                            mm.then_inc(v_turned, 1)
                            pe.wait_ge(ym_ready, OPEN + hd * 2)
                            pe.wait_ge(decay_ready, (l + 1) * HEADS * TT)
                            for s in range(TT):
                                mm = pe.matmul(b_s[:, CAUSAL_AT[s]:CAUSAL_AT[s] + CAUSAL_W[s]],
                                               k_t[:, s * P:(s + 1) * P], q_t[:, T_START[s]:T],
                                               start=(s == 0), stop=(s == TT - 1), skip_group_check=True)
                            mm.then_inc(scores_ready, 1)
                        if i == CX0 + 1:
                            pe.wait_ge(s_w_ready, (hd + 1) * TT)
                            pe.wait_ge(v_n_ready, hd + 1)
                            for t in range(TT):
                                for s in range(t + 1):
                                    mm = pe.matmul(num[:, t, 0:DV + 1], s_w[0:T_SIZE[s], s, t * P:(t + 1) * P],
                                                   v_n[0:T_SIZE[s], s, :], start=(s == 0), stop=(s == t))
                            mm.then_inc(num_ready, 1)
                        if i == CB0 + 1:
                            pe.wait_ge(hm_ready, OPEN + (hd + 1) * TT)
                            for v, bank in enumerate((b_s, b_t)):
                                for t in range(TT):
                                    mm = pe.transpose(bank[:, t * P:t * P + T_SIZE[t]],
                                                      hm[0:T_SIZE[t], t, v * P:(v + 1) * P],
                                                      ident[0:T_SIZE[t], 0:T_SIZE[t]])
                            mm.then_inc(hm_turned, 1)

                pe.wait_ge(y_ready, OPEN + (l + 1) * HEADS)
                for m in range(KT):
                    n = HEADS * PER_HEAD + m
                    if m < 2:
                        pe.wait_ge(sig_c_ready, OPEN + (l + 1) * HEADS * 2)
                    else:
                        pe.wait_ge(h_mixed, l * KT + m - 1)
                    dense(l, n, n % RING, n % 2, y_hi, y_lo)

                mean_square(l * 2 + 1)
                pe.wait_ge(std_ready, l * 2 + 2)
                for t in range(TT):
                    dst = misc[:, t * N_ROUTE:(t + 1) * N_ROUTE]
                    pe.matmul(dst, ones[0:1, :], prm[0:1, C_BROUTE:C_ALL], start=(t == 0), stop=False,
                              skip_group_check=True)
                    for k in range(KT):
                        if t == 0:
                            pe.wait_ge(x_ready, (l * 2 + 1) * KT + k + 1)
                        mm = pe.matmul(dst, norm_buf[:, k, R_START[t]:R_START[t] + P],
                                       prm[:, C_ROUTE + k * N_ROUTE:C_ROUTE + (k + 1) * N_ROUTE],
                                       start=False, stop=(k == KT - 1), skip_group_check=True)
                mm.then_inc(logits_ready, 1)
                pe.wait_ge(gate_n_ready, l + 1)
                for t in range(TT):
                    mm = pe.transpose(misc[0:EXPERTS, R_START[t]:R_START[t] + P], gate_n[:, t, :], ident[:, :])
                mm.then_inc(gate_t_ps, 1)
                with pe.Fori(0, EXPERTS // 2) as pair:
                    for s in range(2):
                        ex = l * EXPERTS + pair * 2 + s
                        pe.wait_ge(gate_b_ready, OPEN + ex)
                        pe.wait_ge(gate_pick_ready, ex + 1)
                        pe.matmul(misc[:, 0:T], ones[0:EXPERTS, :], gate_pick, start=True, stop=True)\
                          .then_inc(gate_b_ps, 1)
                        pe.wait_ge(silu_ready, OPEN + ex * FT)
                        pe.wait_ge(hid_mid, OPEN + ex * FT)
                        for i, bank in enumerate((*acc, b_s, b_t)):
                            slot = s * PER_EXPERT + i
                            pe.wait_ge(m_lo_done, M_RAW + ex * PER_EXPERT + i + 1)
                            for k in range(KT):
                                cols = slice(k * P, (k + 1) * P)
                                mm = three(bank[:, 0:T], m_hi[:, slot, cols], m_lo[:, slot, cols],
                                           x_hi[:, k, :], x_lo[:, k, :], k == 0, k == KT - 1)
                            mm.then_inc(gu_ready, 1)
                        pe.wait_ge(hid_lo_ready, (ex + 1) * FT)
                        pe.wait_ge(m_lo_done, M_RAW + (ex + 1) * PER_EXPERT)
                        for m in range(KT):
                            if m < TT:
                                pe.wait_ge(down_added, OPEN + ex * KT)
                            else:
                                pe.wait_ge(down_added, OPEN + ex * KT + m - TT + 1)
                            for f in range(FT):
                                slot = s * PER_EXPERT + 2 * FT + f
                                cols = slice(m * P, (m + 1) * P)
                                mm = three(num[:, m % TT, 0:T], m_hi[:, slot, cols], m_lo[:, slot, cols],
                                           hid_hi[:, f, :], hid_lo[:, f, :], f == 0, f == FT - 1)
                            mm.then_inc(down_done, 1)
            mean_square(2 * DEPTH)


def lay_out(x, meta_tokens, norm_mix, w_in, b_if, conv_w, mh_gain, w_out, norm_ffn,
            w_group, b_group, w_router, b_router, w_gate, w_up, w_down, norm_final):
    import numpy as np

    def columns(v):
        return np.moveaxis(v.reshape(*v.shape[:-1], -1, P), -1, -2)

    h_in = columns(np.moveaxis(np.concatenate([meta_tokens, x[0]], axis=0), 0, 0))
    h_in = np.transpose(h_in, (1, 2, 0))

    def tiles(w):
        w = w.reshape(DEPTH, KT, P, -1, P)
        return np.transpose(w, (0, 3, 2, 1, 4))

    qk, vw = HEADS * P, D
    at = np.cumsum([0, qk, qk, vw, HEADS, HEADS, vw, D, D, D, D])
    q, k, v, ig, fg, gm, cx, cb, cc, gc = (w_in[:, :, a:b] for a, b in zip(at[:-1], at[1:]))
    q, k, v, gm, cx, cb, cc, gc, wo = (tiles(a) for a in (q, k, v, gm, cx, cb, cc, gc, w_out))
    order = []
    for h in range(HEADS):
        two = slice(2 * h, 2 * h + 2)
        order += [q[:, h:h + 1], k[:, h:h + 1], v[:, two], gm[:, two], cx[:, two], cc[:, two], cb[:, two], gc[:, two]]
    dense_w = np.concatenate([*order, wo], axis=1).reshape(DEPTH, DENSE, P, D)

    def up_tiles(w):
        w = w.reshape(DEPTH, EXPERTS, KT, P, FT, P)
        return np.transpose(w, (0, 1, 4, 3, 2, 5)).reshape(DEPTH, EXPERTS, FT, P, D)

    moe_w = np.concatenate([up_tiles(w_gate), up_tiles(w_up), w_down.reshape(DEPTH, EXPERTS, FT, P, D)], axis=2)
    moe_w = moe_w.reshape(DEPTH, MOE, P, D)

    def rows(w):
        return np.transpose(w.reshape(DEPTH, KT, P, -1), (0, 2, 1, 3)).reshape(DEPTH, P, -1)

    b_gates = np.zeros((DEPTH, P, 1), np.float32)
    b_gates[:, 0:HEADS, 0] = b_if[:, :HEADS]
    b_gates[:, F_ROW:GROWS, 0] = b_if[:, HEADS:]
    b_route = np.zeros((DEPTH, P, N_ROUTE), np.float32)
    b_route[:, 0, :N_GROUPS] = b_group
    b_route[:, 0, N_GROUPS:] = b_router
    conv = np.transpose(columns(conv_w), (0, 2, 1, 3)).reshape(DEPTH, P, -1)
    params = np.concatenate([columns(norm_mix), columns(norm_ffn), columns(mh_gain), conv,
                             rows(np.concatenate([ig, fg], axis=2)),
                             rows(np.concatenate([w_group, w_router], axis=2)), b_gates, b_route], axis=2)
    params = np.transpose(params, (1, 0, 2))
    return {"h_in": h_in, "params": params, "norm_final": columns(norm_final), "dense_w": dense_w, "moe_w": moe_w}


def kernel(**inputs):
    import numpy as _np
    import concourse.bacc as _bacc
    from concourse.bass_utils import run_bass_kernel_spmd as _run

    nc = _bacc.Bacc("TRN2", target_bir_lowering=False, num_devices=1)
    arrays = {name: _np.ascontiguousarray(a) for name, a in
              lay_out(**{name: _np.asarray(a) for name, a in inputs.items()}).items()}
    args = [nc.dram_tensor(name, a.shape, F32, kind="ExternalInput").ap() for name, a in arrays.items()]
    args.append(nc.dram_tensor("out_t", (P, KT, SEQ), F32, kind="ExternalOutput").ap())
    build(nc, *args)
    r = _run(nc, [arrays], core_ids=[0])
    got = r.results[0]["out_t"]
    return _np.ascontiguousarray(_np.transpose(got, (2, 1, 0)).reshape(1, SEQ, D))
```

```python
from contextlib import ExitStack

import concourse.bass as bass
from concourse import mybir

F32 = mybir.dt.float32
F16 = mybir.dt.float16
BF16 = mybir.dt.bfloat16
ALU = mybir.AluOpType
ACT = mybir.ActivationFunctionType
AX = mybir.AxisListType

P = 128
DEPTH = 2
D = 1024
KT = D // P
N_META = 16
SEQ = 256
T = N_META + SEQ
HEADS = 4
DV = D // HEADS
EPS = 1e-6
CONV_K = 3
N_GROUPS, PER_GROUP = 4, 4
EXPERTS = N_GROUPS * PER_GROUP
D_EXPERT = 256
FT = D_EXPERT // P
W_SCALE = 64.0
UNSCALE = 1.0 / W_SCALE
FAR = 1e30

TT = 3
TP = TT * P
T_START = [0, P, 2 * P]
T_SIZE = [P, P, T - 2 * P]
R_START = [0, P, T - P]
CAUSAL_AT = [0, T, T + (T - P)]
CAUSAL_W = [T, T - P, T - 2 * P]
CAUSAL = sum(CAUSAL_W)

Q, K, V0, GM0, CX0, CC0, CB0, GC0, PER_HEAD = 0, 1, 2, 4, 6, 8, 10, 12, 14
DENSE = HEADS * PER_HEAD + KT
RING = 7
SLOTS = 64
PAIRS = EXPERTS // 2
QUADS = EXPERTS // 4
ROUNDS = (T + SLOTS - 1) // SLOTS
KP = KT // 2
GU_TILES = 2 * KP
PER_PAIR = GU_TILES + 2 * FT
MOE = PAIRS * PER_PAIR

C_MIX = 0
C_FFN = C_MIX + KT
C_GAIN = C_FFN + KT
C_CONV = C_GAIN + KT
C_GATE = C_CONV + CONV_K * KT
C_ROUTE = C_GATE + KT * 2 * HEADS
N_ROUTE = N_GROUPS + EXPERTS
C_BIF = C_ROUTE + KT * N_ROUTE
C_BROUTE = C_BIF + 1
C_ALL = C_BROUTE + N_ROUTE
F_ROW = 32
GROWS = F_ROW + HEADS

OPEN = 1


class Chain:

    def __init__(self, eng, sem, base, total):
        self.eng, self.sem, self.base, self.total, self.n = eng, sem, base, total, 0

    def step(self, ins):
        ins.then_inc(self.sem, 1)
        self.n += 1

    def settle(self):
        self.eng.wait_ge(self.sem, self.base + self.n)

    def end(self):
        assert self.n == self.total, (self.sem, self.n, self.total)


def ring_use(l, use, slot):
    return l * ((DENSE - slot + RING - 1) // RING) + use


def build(nc, h_in, params, norm_final, dense_w, moe_w, out):
    with ExitStack() as ctx:
        def sb(name, shape, dt=F32):
            return ctx.enter_context(nc.sbuf_tensor(name, shape, dt))

        def pb(name, shape, dt=F32):
            return ctx.enter_context(nc.psum_tensor(name, shape, dt))

        def sem(name):
            return ctx.enter_context(nc.semaphore(name))

        h_t = sb("h_t", [P, KT, T])
        norm_buf = sb("norm_buf", [P, KT, T])
        x_parts = sb("x_parts", [P, 2, KT, T], F16)
        x_hi, x_lo = x_parts[:, 0, :, :], x_parts[:, 1, :, :]
        y_hi = sb("y_hi", [P, KT, T], F16)
        y_lo = sb("y_lo", [P, KT, T], F16)
        rstd = sb("rstd", [P, T])
        raw = sb("raw", [P, RING, D])
        w_hi = sb("w_hi", [P, RING, D], F16)
        w_lo = sb("w_lo", [P, RING, D], F16)
        m_raw = sb("m_raw", [P, 2 * GU_TILES + 2 * FT, D])
        prm_all = sb("prm_all", [P, DEPTH, C_ALL])
        prm = sb("prm", [P, C_ALL])
        fin_gain = sb("fin_gain", [P, KT])
        gate_hi = sb("gate_hi", [P, KT, GROWS], F16)
        gate_lo = sb("gate_lo", [P, KT, GROWS], F16)
        ones = sb("ones", [P, P])
        ident = sb("ident", [P, P])
        ident_b = sb("ident_b", [P, P], BF16)
        ahead = sb("ahead", [P, CAUSAL], BF16)
        eps = sb("eps", [P, 1])
        half = sb("half", [P, TT])
        a_floor = sb("a_floor", [P, TP])
        a_col = sb("a_col", [P, TT, GROWS])
        scratch = sb("scratch", [P, HEADS * CAUSAL])
        cx, cv, ym = (scratch[:, i * 2 * T:(i + 1) * 2 * T].rearrange("p (a t) -> p a t", a=2) for i in range(3))
        g_pick = scratch[0:HEADS, :].rearrange("p (h c) -> p h c", h=HEADS)
        norm_flat = norm_buf[:, :, :].rearrange("p k t -> p (k t)")
        decay = norm_flat[:, 0:HEADS * CAUSAL].rearrange("p (h c) -> p h c", h=HEADS)
        q_t = norm_flat[:, HEADS * CAUSAL:HEADS * CAUSAL + T]
        k_t = sb("k_t", [P, TP])
        v_flat = sb("v_flat", [P, TT * DV])
        v_t = v_flat[:, :].rearrange("p (v t) -> p v t", v=2)
        hm = v_flat[:, :].rearrange("p (t d) -> p t d", t=TT)
        v_n = sb("v_n", [P, TT, DV + 1])
        s_w = sb("s_w", [P, TT, TP])
        sig_m = sb("sig_m", [P, 2, T])
        sig_c = sb("sig_c", [P, 2, T])
        i_gate, f_sum, g_max, m_row = (b[0:HEADS, j, :] for b in (sig_m, sig_c) for j in range(2))
        f_gate, f_abs, f_exp, f_log = (b[F_ROW:GROWS, j, :] for b in (sig_m, sig_c) for j in range(2))
        u = sb("u", [P, 2, T + CONV_K - 1])
        ssq = sb("ssq", [P, TT])
        den = sb("den", [P, TT])
        stat = sb("stat", [P, 6, TT])
        lg = sb("lg", [P, TT, N_ROUTE])
        small = sb("small", [P, 24, TT])
        iota_e = sb("iota_e", [P, TT, 4])
        gate_n = sb("gate_n", [P, TT, EXPERTS])
        sel = sb("sel", [P, TT, EXPERTS], F16)
        pos1 = sb("pos1", [P, TT, EXPERTS])
        place = sb("place", [P, SLOTS])
        before = sb("before", [P, P], F16)
        one_h = sb("one_h", [P, P], F16)
        ident_h = sb("ident_h", [P, P], F16)
        limits = sb("limits", [P, ROUNDS])
        busiest = sb("busiest", [P, 1])
        needed = sb("needed", [P, ROUNDS])
        rounds_n = sb("rounds_n", [P, 1])
        rounds_f = sb("rounds_f", [P, 1])
        opened = sb("opened", [1, 16])
        rounds_at = sb("rounds_at", [P, DEPTH + 1], mybir.dt.int32)
        fresh = sb("fresh", [P, TT])
        gate_q = sb("gate_q", [P, 2, TT, 4], F16)
        slot_gate = sb("slot_gate", [P, 2])
        xn_hi = w_hi[:, RING - TT:, :]
        xn_lo = w_lo[:, RING - TT:, :]

        def gu_slot(p, i):
            return m_raw[:, p * GU_TILES + i, :]

        def down_slot(p, i):
            return m_raw[:, 2 * GU_TILES + i, :] if p == 0 else raw[:, i, :]

        xg = x_parts[:, :, :, :].rearrange("p a k t -> p (a k t)").bitcast(F32)[:, 0:KT * 4 * SLOTS]\
            .rearrange("p (k s) -> p k s", k=KT)
        sg = sig_m[:, :, :].rearrange("p a t -> p (a t)")[:, 0:2 * D_EXPERT].rearrange("p (a f) -> p a f", a=2)
        hid = sig_c[:, :, :].rearrange("p a t -> p (a t)")[:, 0:2 * D_EXPERT].rearrange("p (a f) -> p a f", a=2)
        hid_t = scratch[:, 0:2 * FT * P].rearrange("p (a f s) -> p a f s", a=2, f=FT)
        RT_AT = 2 * FT * P
        PICK_AT = RT_AT + 12 * TT * EXPERTS
        rt = scratch[:, RT_AT:PICK_AT].rearrange("p (i t e) -> p i t e", i=12, t=TT)
        pick = scratch[:, PICK_AT:PICK_AT + TT * 2 * SLOTS].bitcast(F16).rearrange("p (t s) -> p t s", t=TT)
        back = v_flat[:, 0:T].bitcast(F16).rearrange("p (a t) -> p a t", a=2)
        ys_hi = y_hi[:, :, :].rearrange("p k t -> p (k t)")[:, 0:2 * D].rearrange("p (a d) -> p a d", a=2)
        ys_lo = y_lo[:, :, :].rearrange("p k t -> p (k t)")[:, 0:2 * D].rearrange("p (a d) -> p a d", a=2)

        acc = [pb(f"acc{i}", [P, 512]) for i in range(2)]
        b_s = pb("b_s", [P, 512])
        b_t = pb("b_t", [P, 512])
        num = pb("num", [P, TT, 512])
        misc = pb("misc", [P, 512])
        misc_h = misc[:, :].bitcast(F16)
        BACK_AT = 64

        h_loaded = sem("h_loaded")
        prm_loaded = sem("prm_loaded")
        consts = sem("consts")
        zeroed = sem("zeroed")
        padded = sem("padded")
        raw_landed = [sem(f"raw_landed{i}") for i in range(RING)]
        hi_done = sem("hi_done")
        lo_done = sem("lo_done")
        tiles_done = sem("tiles_done")
        gu_landed = [[sem(f"gu_landed{p}_{i}") for i in range(GU_TILES)] for p in range(2)]
        down_landed = [[sem(f"down_landed{p}_{i}") for i in range(2 * FT)] for p in range(2)]
        gu_done = sem("gu_done")
        down_done = sem("down_done")
        prep_done = sem("prep_done")
        sq_ready = sem("sq_ready")
        ms_ready = sem("ms_ready")
        std_ready = sem("std_ready")
        rstd_ready = sem("rstd_ready")
        x_ready = sem("x_ready")
        x_hi_ready = sem("x_hi_ready")
        x_lo_ready = sem("x_lo_ready")
        gates_ready = sem("gates_ready")
        gate_step = sem("gate_step")
        f_abs_ready = sem("f_abs_ready")
        f_exp_ready = sem("f_exp_ready")
        f_log_ready = sem("f_log_ready")
        m_row_ready = sem("m_row_ready")
        floor_ready = sem("floor_ready")
        a_ready = sem("a_ready")
        pick_ready = sem("pick_ready")
        a_col_ps = sem("a_col_ps")
        a_col_ready = sem("a_col_ready")
        arg_ready = sem("arg_ready")
        decay_ready = sem("decay_ready")
        qkv_ready = sem("qkv_ready")
        v_turned = sem("v_turned")
        v_n_ready = sem("v_n_ready")
        scores_ready = sem("scores_ready")
        s_w_ready = sem("s_w_ready")
        num_ready = sem("num_ready")
        ssq_ready = sem("ssq_ready")
        head_step = sem("head_step")
        var_ready = sem("var_ready")
        pow_ready = sem("pow_ready")
        f_ready = sem("f_ready")
        hm_ready = sem("hm_ready")
        hm_turned = sem("hm_turned")
        sig_m_ready = sem("sig_m_ready")
        sig_c_ready = sem("sig_c_ready")
        cx_ready = sem("cx_ready")
        y_ready = sem("y_ready")
        ym_ready = sem("ym_ready")
        cc_read = sem("cc_read")
        cb_read = sem("cb_read")
        h_mixed = sem("h_mixed")
        logits_ready = sem("logits_ready")
        route_step = sem("route_step")
        exp_in_ready = sem("exp_in_ready")
        exp_ready = sem("exp_ready")
        xn_turned = sem("xn_turned")
        xn_hi_ready = sem("xn_hi_ready")
        xn_lo_ready = sem("xn_lo_ready")
        sel_ready = sem("sel_ready")
        pos_ps = sem("pos_ps")
        pos_ready = sem("pos_ready")
        rounds_ready = sem("rounds_ready")
        gate_q_ready = sem("gate_q_ready")
        pick_ready_q = sem("pick_ready_q")
        gathered = sem("gathered")
        xg_ready = sem("xg_ready")
        slots_ps = sem("slots_ps")
        slot_gate_ready = sem("slot_gate_ready")
        back_ready = sem("back_ready")
        sg_ready = sem("sg_ready")
        silu_ready = sem("silu_ready")
        hid_ready = sem("hid_ready")
        hid_turned = sem("hid_turned")
        hid_t_ready = sem("hid_t_ready")
        ys_hi_ready = sem("ys_hi_ready")
        ys_lo_ready = sem("ys_lo_ready")
        combined = sem("combined")
        h_added = sem("h_added")
        out_stored = sem("out_stored")

        wide = [num[:, 0, :], num[:, 1, :], num[:, 2, :], acc[0][:, :], acc[1][:, :], b_s[:, :]]

        def y_ps(p, dh):
            return num[:, dh, :] if p == 0 else acc[dh][:, :]

        def rounds_before(eng, l):
            if eng is not nc.vector:
                eng.wait_ge(rounds_ready, OPEN + l)
            return eng.value_load(rounds_at[0:1, bass.ds(l, 1)], min_val=0, max_val=DEPTH * ROUNDS)

        block = ctx.enter_context(nc.Block())

        N_CONST = 11

        @block.sync
        def _(sp):
            sp.dma_start(h_t[:, :, :], h_in).then_inc(h_loaded, 16)
            sp.dma_start(prm_all[:, :, :], params).then_inc(prm_loaded, 16)
            sp.dma_start(fin_gain[:, :], norm_final).then_inc(prm_loaded, 16)

            def load_dense(l, n, slot):
                sp.wait_ge(lo_done, l * DENSE + n + 1)
                sp.dma_start(raw[:, slot, :], dense_w[l, n]).then_inc(raw_landed[slot], 16)

            def load_gu(l, q, qd, p):
                for i in range(GU_TILES):
                    sp.wait_ge(gu_done, (qd * 2 + p) * KP + i // 2 + 1)
                    sp.dma_start(gu_slot(p, i), moe_w[l, (q * 2 + p) * PER_PAIR + i]).then_inc(gu_landed[p][i], 16)

            def load_down(l, q, qd, p):
                for i in range(2 * FT):
                    sp.wait_ge(down_done, (qd * 2 + p) * FT + i // 2 + 1)
                    sp.dma_start(down_slot(p, i), moe_w[l, (q * 2 + p) * PER_PAIR + GU_TILES + i])\
                      .then_inc(down_landed[p][i], 16)

            def load_quad(l, q, qd):
                load_gu(l, q, qd, 0)
                load_gu(l, q, qd, 1)
                load_down(l, q, qd, 0)
                load_down(l, q, qd, 1)

            with sp.Fori(0, DEPTH) as l:
                first = rounds_before(sp, l)
                for n in range(RING):
                    if n == 0:
                        sp.wait_ge(down_done, 2 * FT + first * QUADS * 2 * FT)
                    load_dense(l, n, n)
                load_gu(l, 0, first * QUADS, 0)
                load_down(l, 0, first * QUADS, 0)
                load_gu(l, 0, first * QUADS, 1)
                with sp.Fori(0, HEADS) as h:
                    for i in range(PER_HEAD):
                        load_dense(l, RING + h * PER_HEAD + i, i % RING)
                load_dense(l, DENSE - 1, (DENSE - 1) % RING)
                sp.wait_ge(lo_done, RING + (l + 1) * DENSE)
                load_down(l, 0, first * QUADS, 1)
                with sp.Fori(1, QUADS) as q:
                    load_quad(l, q, first * QUADS + q)
                last = rounds_before(sp, l + 1)
                with sp.If(last > first + 1):
                    with sp.Fori(first + 1, last) as rd:
                        with sp.Fori(0, QUADS) as q:
                            load_quad(l, q, rd * QUADS + q)
            for k in range(KT):
                sp.wait_ge(x_ready, 2 * DEPTH * KT + k + 1)
                sp.dma_start(out[:, k, :], norm_buf[:, k, N_META:]).then_inc(out_stored, 16)
            sp.wait_ge(out_stored, 16 * KT)

        @block.gpsimd
        def _(pool):
            pool.memset(ones[:, :], 1.0).then_inc(consts, 1)
            pool.memset(ident[:, :], 0.0).then_inc(zeroed, 1)
            pool.memset(ahead[:, :], 0.0).then_inc(zeroed, 1)
            pool.wait_ge(zeroed, 2)
            pool.affine_select(out=ident[:, :], in_=ident[:, :], compare_op=ALU.not_equal, fill=1.0,
                               base=0, pattern=[[-1, P]], channel_multiplier=1).then_inc(consts, 1)
            pool.wait_ge(consts, 2)
            pool.tensor_copy(ident_b[:, :], ident[:, :]).then_inc(consts, 1)
            for at, w in zip(CAUSAL_AT, CAUSAL_W):
                pool.affine_select(out=ahead[:, at:at + w], in_=ahead[:, at:at + w], compare_op=ALU.is_ge,
                                   fill=FAR, base=0, pattern=[[1, w]], channel_multiplier=-1).then_inc(consts, 1)
            pool.memset(eps[:, :], EPS).then_inc(consts, 1)
            pool.memset(half[:, :], -0.5).then_inc(consts, 1)
            pool.tensor_copy(ident_h[:, :], ident[:, :]).then_inc(consts, 1)
            pool.memset(one_h[:, :], 1.0).then_inc(zeroed, 1)
            pool.memset(fresh[:, :], 1.0).then_inc(zeroed, 1)
            pool.wait_ge(zeroed, 4)
            pool.affine_select(out=before[:, :], in_=one_h[:, :], compare_op=ALU.is_ge, fill=0.0,
                               base=-1, pattern=[[1, P]], channel_multiplier=-1).then_inc(consts, 1)
            pool.affine_select(out=fresh[:, TT - 1:TT], in_=fresh[:, TT - 1:TT], compare_op=ALU.is_ge, fill=0.0,
                               base=-(P - T_SIZE[TT - 1]), pattern=[[0, 1]], channel_multiplier=1)\
                .then_inc(consts, 1)
            with pool.Fori(0, DEPTH) as l:
                with pool.Fori(0, HEADS) as h:
                    hd = l * HEADS + h
                    pool.wait_ge(var_ready, hd + 1)
                    pool.tensor_tensor(stat[:, 4, :], stat[:, 3, :], half[:, :], ALU.pow).then_inc(pow_ready, 1)

        @block.scalar
        def _(act):
            def hi_dense(l, n, slot, use):
                act.wait_ge(raw_landed[slot], (ring_use(l, use, slot) + 1) * 16)
                act.wait_ge(tiles_done, l * DENSE + n + 1)
                act.activation(w_hi[:, slot, :], raw[:, slot, :], ACT.Copy, scale=W_SCALE).then_inc(hi_done, 1)

            def norm(i):
                for k in range(KT):
                    act.activation(norm_buf[:, k, :], h_t[:, k, :], ACT.Square).then_inc(sq_ready, 1)
                act.wait_ge(ms_ready, i + 1)
                act.activation(rstd[:, :], misc[:, 0:T], ACT.Sqrt, bias=eps[:, 0:1], scale=1.0 / D)\
                   .then_inc(std_ready, 1)

            def norm_hi(l):
                for k in range(KT):
                    act.wait_ge(x_ready, 2 * l * KT + k + 1)
                    act.activation(x_hi[:, k, :], norm_buf[:, k, :], ACT.Copy).then_inc(x_hi_ready, 1)

            def take_gathered(qd, side):
                for kp in (2 * side, 2 * side + 1):
                    act.wait_ge(gathered, qd * KP + kp + 1)
                    act.activation(xg[:, 2 * kp:2 * kp + 2, :],
                                   [b_s, b_t][kp % 2][:, :].rearrange("p (k s) -> p k s", k=2), ACT.Copy)\
                       .then_inc(xg_ready, 1)

            act.wait_ge(h_loaded, 16)
            act.wait_ge(consts, N_CONST)
            with act.Fori(0, DEPTH) as l:
                first = rounds_before(act, l)
                for n in range(3):
                    hi_dense(l, n, n, 0)
                act.wait_ge(h_added, OPEN + first * QUADS * KT)
                norm(l * 2)
                norm_hi(l)
                act.wait_ge(f_abs_ready, l + 1)
                act.activation(f_exp, f_abs, ACT.Exp, scale=-1.0)\
                   .then_inc(f_exp_ready, 1)
                act.wait_ge(f_exp_ready, l + 1)
                act.activation(f_log, f_exp, ACT.Ln, bias=1.0)\
                   .then_inc(f_log_ready, 1)
                act.wait_ge(m_row_ready, l + 1)
                act.activation(a_floor[F_ROW:GROWS, 0:T], m_row, ACT.Exp, scale=-1.0)\
                   .then_inc(floor_ready, 1)
                act.wait_ge(a_col_ready, l + 1)
                for h in range(HEADS):
                    act.wait_ge(arg_ready, l * HEADS + h + 1)
                    for s in range(TT):
                        at, w, sz = CAUSAL_AT[s], CAUSAL_W[s], P
                        act.activation(decay[:, h, at:at + w], [b_s, b_t][h % 2][:, at:at + w], ACT.Exp,
                                       bias=a_col[:, s, h:h + 1], scale=-1.0).then_inc(decay_ready, 1)

                with act.Fori(0, HEADS) as h:
                    hd = l * HEADS + h
                    tile0 = l * DENSE + h * PER_HEAD
                    for i in range(PER_HEAD):
                        nxt = i + 3
                        hi_dense(l, h * PER_HEAD + nxt, nxt % RING, h * 2 + nxt // RING)
                        if i == V0 + 3:
                            act.wait_ge(v_turned, hd + 1)
                            act.activation(v_n[:, :, 0:DV], num[:, :, 0:DV], ACT.Copy).then_inc(v_n_ready, 1)
                        if i == CC0:
                            act.wait_ge(num_ready, hd + 1)
                            for t in range(TT):
                                act.activation(hm[:, t, :], num[:, t, 0:DV], ACT.Square,
                                               accum_out=ssq[:, t:t + 1]).then_inc(ssq_ready, 1)
                            act.activation(den[:, :], num[:, :, DV], ACT.Copy).then_inc(ssq_ready, 1)
                        if i == CC0 + 1:
                            act.wait_ge(f_ready, hd + 1)
                            for t in range(TT):
                                act.activation(hm[:, t, :], num[:, t, 0:DV], ACT.Copy,
                                               scale=stat[:, 5, t:t + 1]).then_inc(hm_ready, 1)
                        if i in (GM0, GM0 + 1, CX0, CX0 + 1, GC0, GC0 + 1):
                            act.wait_ge(tiles_done, RING + tile0 + i + 1)
                            if i == GM0:
                                act.wait_ge(ym_ready, OPEN + hd * 2)
                            if i == GC0:
                                act.wait_ge(y_ready, OPEN + hd)
                            dst, func, ready = {GM0: (sig_m, ACT.Sigmoid, sig_m_ready), CX0: (cx, ACT.Copy, cx_ready),
                                                GC0: (sig_c, ACT.Sigmoid, sig_c_ready)}[i - i % 2]
                            act.activation(dst[:, i % 2, :], acc[i % 2][:, 0:T], func, scale=UNSCALE)\
                               .then_inc(ready, 1)
                for m in range(KT):
                    if m + 3 < KT:
                        n = HEADS * PER_HEAD + m + 3
                        hi_dense(l, n, n % RING, n // RING)

                act.wait_ge(h_mixed, (l + 1) * KT)
                norm(l * 2 + 1)
                for t in range(TT):
                    for half_d in range(2):
                        i = t * 2 + half_d
                        act.wait_ge(xn_turned, l * 2 * TT + i + 1)
                        act.activation(xn_hi[:, t, half_d * 512:(half_d + 1) * 512], wide[i][:, :], ACT.Copy)\
                           .then_inc(xn_hi_ready, 1)
                act.wait_ge(exp_in_ready, l + 1)
                act.activation(small[:, 8:13, :], small[:, 0:5, :], ACT.Exp).then_inc(exp_ready, 1)

                last = rounds_before(act, l + 1)
                take_gathered(first * QUADS, 0)
                take_gathered(first * QUADS, 1)
                with act.Fori(first, last) as rd, act.Fori(0, QUADS) as q:
                    qd = rd * QUADS + q
                    for p in range(2):
                        pr = qd * 2 + p
                        act.wait_ge(gu_done, 2 * KP + (pr + 1) * KP)
                        act.activation(sg[:, p, :], acc[p][:, 0:D_EXPERT], ACT.Sigmoid).then_inc(sg_ready, 1)
                        act.wait_ge(hid_turned, pr + 1)
                        act.activation(hid_t[:, p, :, :],
                                       num[:, 2, p * FT * P:(p + 1) * FT * P].rearrange("p (f s) -> p f s", f=FT),
                                       ACT.Copy).then_inc(hid_t_ready, 1)
                    for p in range(2):
                        pr = qd * 2 + p
                        with act.If(qd + 1 < last * QUADS):
                            take_gathered(qd + 1, p)
                        if p == 0:
                            act.wait_ge(combined, OPEN + qd * KT)
                        act.wait_ge(down_done, 2 * FT + (pr + 1) * FT)
                        for dh in range(2):
                            act.activation(ys_hi[:, p, dh * 512:(dh + 1) * 512], y_ps(p, dh), ACT.Copy)\
                               .then_inc(ys_hi_ready, 1)
            act.wait_ge(h_added, OPEN + rounds_before(act, DEPTH) * QUADS * KT)
            norm(2 * DEPTH)

        PREP, GATE, HEAD, ROUTE = 5, 9, 14, 38

        @block.vector
        def _(dve):
            init = Chain(dve, padded, 0, 10)
            init.step(dve.memset(k_t[:, :], 0.0))
            init.step(dve.memset(v_t[:, :, :], 0.0))
            init.step(dve.memset(s_w[:, :, :], 0.0))
            init.step(dve.memset(v_n[:, :, DV:DV + 1], 1.0))
            init.step(dve.memset(u[:, :, 0:CONV_K - 1], 0.0))
            init.step(dve.memset(a_floor[:, :], 1.0))
            init.step(dve.memset(gate_hi[:, :, :], 0.0))
            init.step(dve.memset(gate_lo[:, :, :], 0.0))
            init.step(dve.memset(place[:, :], 1.0))
            init.settle()
            init.step(dve.tensor_tensor_scan(place[:, :], place[:, :], place[:, :], 0.0, ALU.mult, ALU.add))
            init.end()
            for b in range(ROUNDS):
                dve.memset(limits[:, b:b + 1], float(b * SLOTS) if b else -1.0).then_inc(padded, 1)
            dve.memset(rounds_f[:, :], 0.0).then_inc(padded, 1)
            dve.memset(rounds_at[:, :], 0).then_inc(rounds_ready, OPEN)
            dve.memset(opened[0:1, 0:1], 0.0).then_inc(lo_done, RING)
            dve.memset(opened[0:1, 1:2], 0.0).then_inc(tiles_done, RING)
            dve.memset(opened[0:1, 2:3], 0.0).then_inc(gu_done, 2 * KP)
            dve.memset(opened[0:1, 3:4], 0.0).then_inc(down_done, 2 * FT)
            for n, s in enumerate((ym_ready, sig_c_ready, hm_ready, y_ready, h_added, combined, back_ready,
                                   ys_lo_ready)):
                dve.memset(opened[0:1, 4 + n:5 + n], 0.0).then_inc(s, OPEN)
            for e in range(4):
                dve.memset(iota_e[:, :, e:e + 1], float(e)).then_inc(padded, 1)
            dve.wait_ge(padded, 10 + 4 + ROUNDS + 1)
            dve.wait_ge(prm_loaded, 32)
            dve.wait_ge(consts, N_CONST)
            dve.wait_ge(h_loaded, 16)

            def lo_dense(l, n, slot):
                dve.wait_ge(hi_done, l * DENSE + n + 1)
                dve.scalar_tensor_tensor(w_lo[:, slot, :], raw[:, slot, :], W_SCALE, w_hi[:, slot, :],
                                         ALU.mult, ALU.subtract).then_inc(lo_done, 1)

            def norm(i, gain, l=None):
                dve.wait_ge(std_ready, i + 1)
                dve.reciprocal(rstd[:, :], rstd[:, :]).then_inc(rstd_ready, 1)
                dve.wait_ge(rstd_ready, i + 1)

                def low(k):
                    dve.wait_ge(x_hi_ready, l * KT + k + 1)
                    dve.tensor_tensor(x_lo[:, k, :], norm_buf[:, k, :], x_hi[:, k, :], ALU.subtract)\
                       .then_inc(x_lo_ready, 1)
                for k in range(KT):
                    dve.scalar_tensor_tensor(norm_buf[:, k, :], h_t[:, k, :], gain[:, k:k + 1], rstd[:, :],
                                             ALU.mult, ALU.mult).then_inc(x_ready, 1)
                    if l is not None and k:
                        low(k - 1)
                if l is not None:
                    low(KT - 1)

            def fill_slots(l, qd, q):
                four = bass.ds(q * 4, 4)
                dve.wait_ge(pos_ready, qd + l + 1)
                dve.tensor_tensor(pick[:, :, :].rearrange("p t (e s) -> p t e s", e=4),
                                  place[:, :].unsqueeze(1).unsqueeze(1).broadcast_to([P, TT, 4, SLOTS]),
                                  pos1[:, :, four].unsqueeze(3).broadcast_to([P, TT, 4, SLOTS]), ALU.is_equal)\
                   .then_inc(pick_ready_q, 1)
                dve.wait_ge(pick_ready_q, qd + 1)
                dve.tensor_scalar(pos1[:, :, four], pos1[:, :, four], float(-SLOTS), None, ALU.add)\
                   .then_inc(pos_ready, 1)
                dve.tensor_scalar(gate_q[:, 0, :, :], gate_n[:, :, four], 1.0, None, ALU.mult)\
                   .then_inc(gate_q_ready, 1)
                dve.wait_ge(gate_q_ready, qd * 2 + 1)
                dve.tensor_tensor(gate_q[:, 1, :, :], gate_n[:, :, four], gate_q[:, 0, :, :], ALU.subtract)\
                   .then_inc(gate_q_ready, 1)

            dve.wait_ge(rounds_ready, OPEN)
            with dve.Fori(0, DEPTH) as l:
                first = rounds_before(dve, l)
                prep = Chain(dve, prep_done, l * PREP, PREP)
                prep.step(dve.tensor_scalar(prm[:, :], prm_all[:, l, :], 1.0, None, ALU.mult))
                prep.settle()
                gw = prm[:, C_GATE:C_ROUTE].rearrange("p (k g) -> p k g", k=KT)
                for g, row in ((0, 0), (HEADS, F_ROW)):
                    prep.step(dve.tensor_scalar(gate_hi[:, :, row:row + HEADS], gw[:, :, g:g + HEADS], W_SCALE, None,
                                                ALU.mult))
                prep.settle()
                for g, row in ((0, 0), (HEADS, F_ROW)):
                    prep.step(dve.scalar_tensor_tensor(gate_lo[:, :, row:row + HEADS], gw[:, :, g:g + HEADS], W_SCALE,
                                                       gate_hi[:, :, row:row + HEADS], ALU.mult, ALU.subtract))
                prep.end()
                lo_dense(l, 0, 0)
                lo_dense(l, 1, 1)
                norm(l * 2, prm[:, C_MIX:C_MIX + KT], l)

                dve.wait_ge(gates_ready, l + 1)
                g = Chain(dve, gate_step, l * GATE, GATE)
                g.step(dve.tensor_scalar(i_gate, misc[0:HEADS, 0:T], UNSCALE, prm[0:HEADS, C_BIF:C_BIF + 1],
                                         ALU.mult, ALU.add))
                g.step(dve.tensor_scalar(f_gate, misc[F_ROW:GROWS, 0:T], UNSCALE,
                                         prm[F_ROW:GROWS, C_BIF:C_BIF + 1], ALU.mult, ALU.add))
                g.settle()
                dve.scalar_tensor_tensor(f_abs, f_gate, -1.0, f_gate, ALU.mult, ALU.max)\
                   .then_inc(f_abs_ready, 1)
                dve.wait_ge(f_log_ready, l + 1)
                g.step(dve.scalar_tensor_tensor(f_log, f_gate, 0.0,
                                                f_log, ALU.min, ALU.subtract))
                g.settle()
                g.step(dve.tensor_tensor_scan(f_sum, ones[F_ROW:GROWS, 0:1].broadcast_to([HEADS, T]), f_log, 0.0,
                                              ALU.mult, ALU.add))
                g.settle()
                g.step(dve.tensor_tensor(a_floor[0:HEADS, 0:T], i_gate, f_sum, ALU.subtract))
                g.settle()
                g.step(dve.tensor_tensor_scan(g_max, a_floor[0:HEADS, 0:T], a_floor[0:HEADS, 0:T], 0.0,
                                              ALU.max, ALU.max))
                g.settle()
                dve.tensor_tensor(m_row, f_sum, g_max, ALU.add).then_inc(m_row_ready, 1)
                for s in range(TT):
                    at, w = CAUSAL_AT[s], CAUSAL_W[s]
                    g.step(dve.tensor_copy(g_pick[:, 0, at:at + w], g_max[:, T_START[s]:T]))
                g.settle()
                for h in reversed(range(HEADS)):
                    dve.tensor_scalar(g_pick[:, h, :], g_pick[:, 0, :], ident[0:HEADS, h:h + 1], None, ALU.mult)\
                       .then_inc(pick_ready, 1)
                g.end()
                dve.wait_ge(a_col_ps, l + 1)
                dve.tensor_copy(a_col[:, :, :], misc[:, 0:TP].rearrange("p (t g) -> p t g", t=TT)[:, :, 0:GROWS])\
                   .then_inc(a_col_ready, 1)

                with dve.Fori(0, HEADS) as h:
                    hd = l * HEADS + h
                    tile0 = l * DENSE + h * PER_HEAD
                    c = Chain(dve, head_step, hd * HEAD, HEAD)
                    for i in range(PER_HEAD):
                        nxt = i + 2
                        lo_dense(l, h * PER_HEAD + nxt, nxt % RING)
                        b, ct = acc[i % 2][:, 0:T], i % 2
                        if i in (Q, K, V0, V0 + 1, CC0, CC0 + 1, CB0, CB0 + 1):
                            dve.wait_ge(tiles_done, RING + tile0 + i + 1)
                        if i in (Q, K, V0, V0 + 1):
                            dst = {Q: q_t[:, :], K: k_t[:, 0:T], V0: v_t[:, 0, 0:T], V0 + 1: v_t[:, 1, 0:T]}[i]
                            dve.tensor_scalar(dst, b, UNSCALE, None, ALU.mult).then_inc(qkv_ready, 1)
                        if i == GM0 + 1:
                            dve.wait_ge(scores_ready, hd + 1)
                            dve.wait_ge(decay_ready, (l + 1) * HEADS * TT)
                            for s in range(TT):
                                at, w = CAUSAL_AT[s], CAUSAL_W[s]
                                dve.scalar_tensor_tensor(s_w[:, s, T_START[s]:T], b_s[:, at:at + w], P ** -0.5,
                                                         decay[:, h, at:at + w], ALU.mult, ALU.mult)\
                                   .then_inc(s_w_ready, 1)
                        if i in (CC0, CC0 + 1):
                            dve.wait_ge(cx_ready, hd * 2 + ct + 1)
                            dve.scalar_tensor_tensor(u[:, ct, CONV_K - 1:], b, UNSCALE, cx[:, ct, :],
                                                     ALU.mult, ALU.mult).then_inc(cc_read, 1)
                            dve.wait_ge(cc_read, hd * 2 + ct + 1)
                            tap = [prm[:, C_CONV + j * KT:C_CONV + (j + 1) * KT] for j in range(CONV_K)]
                            c.step(dve.tensor_scalar(cv[:, ct, :], u[:, ct, 0:T], tap[0][:, bass.ds(h * 2 + ct, 1)],
                                                     None, ALU.mult))
                            for j in range(1, CONV_K):
                                c.settle()
                                c.step(dve.scalar_tensor_tensor(cv[:, ct, :], u[:, ct, j:j + T],
                                                                tap[j][:, bass.ds(h * 2 + ct, 1)], cv[:, ct, :],
                                                                ALU.mult, ALU.add))
                        if i == CC0:
                            dve.wait_ge(ssq_ready, (hd + 1) * (TT + 1))
                            c.step(dve.scalar_tensor_tensor(stat[:, 0, :], den[:, :], -1.0, den[:, :],
                                                            ALU.mult, ALU.max))
                            c.settle()
                            dve.wait_ge(a_col_ready, l + 1)
                            c.step(dve.tensor_tensor(stat[:, 0, :], stat[:, 0, :],
                                                     a_col[:, :, bass.ds(F_ROW + h, 1)].rearrange("p t o -> p (t o)"),
                                                     ALU.max))
                            c.settle()
                            c.step(dve.reciprocal(stat[:, 1, :], stat[:, 0, :]))
                            c.settle()
                            c.step(dve.tensor_tensor(stat[:, 2, :], ssq[:, :], stat[:, 1, :], ALU.mult))
                            c.settle()
                            c.step(dve.tensor_tensor(stat[:, 2, :], stat[:, 2, :], stat[:, 1, :], ALU.mult))
                            c.settle()
                            dve.tensor_scalar(stat[:, 3, :], stat[:, 2, :], 1.0 / DV, EPS, ALU.mult, ALU.add)\
                               .then_inc(var_ready, 1)
                            dve.wait_ge(pow_ready, hd + 1)
                            dve.tensor_tensor(stat[:, 5, :], stat[:, 1, :], stat[:, 4, :], ALU.mult)\
                               .then_inc(f_ready, 1)
                        if i in (CB0, CB0 + 1):
                            c.settle()
                            dve.scalar_tensor_tensor(cv[:, ct, :], b, UNSCALE, cv[:, ct, :],
                                                     ALU.mult, ALU.mult).then_inc(cb_read, 1)
                        if i == GC0:
                            dve.wait_ge(hm_turned, hd + 1)
                            dve.wait_ge(sig_m_ready, (hd + 1) * 2)
                            for v, bank in enumerate((b_s, b_t)):
                                dve.scalar_tensor_tensor(ym[:, v, :], bank[:, 0:T],
                                                         prm[:, bass.ds(C_GAIN + h * 2 + v, 1)],
                                                         sig_m[:, v, :], ALU.mult, ALU.mult).then_inc(ym_ready, 1)
                    dve.wait_ge(sig_c_ready, OPEN + (hd + 1) * 2)
                    dve.wait_ge(cb_read, (hd + 1) * 2)
                    c.step(dve.tensor_tensor(cv[:, :, :], cv[:, :, :], sig_c[:, :, :], ALU.mult))
                    c.settle()
                    dve.wait_ge(ym_ready, OPEN + (hd + 1) * 2)
                    c.step(dve.tensor_tensor(ym[:, :, :], cv[:, :, :], ym[:, :, :], ALU.add))
                    c.settle()
                    c.step(dve.tensor_scalar(y_hi[:, bass.ds(h * 2, 2), :], ym[:, :, :], 1.0, None, ALU.mult))
                    c.settle()
                    dve.tensor_tensor(y_lo[:, bass.ds(h * 2, 2), :], ym[:, :, :], y_hi[:, bass.ds(h * 2, 2), :],
                                      ALU.subtract).then_inc(y_ready, 1)
                    c.end()

                for m in range(KT):
                    n = HEADS * PER_HEAD + m
                    if m + 2 < KT:
                        lo_dense(l, n + 2, (n + 2) % RING)
                    dve.wait_ge(tiles_done, RING + l * DENSE + n + 1)
                    dve.scalar_tensor_tensor(h_t[:, m, :], acc[n % 2][:, 0:T], UNSCALE, h_t[:, m, :],
                                             ALU.mult, ALU.add).then_inc(h_mixed, 1)

                dve.wait_ge(h_mixed, (l + 1) * KT)
                norm(l * 2 + 1, prm[:, C_FFN:C_FFN + KT])

                r = Chain(dve, route_step, l * ROUTE, ROUTE)

                def then(ins):
                    r.step(ins)
                    r.settle()

                dve.wait_ge(logits_ready, l + 1)
                then(dve.tensor_copy(lg[:, :, :], misc[:, 0:TT * N_ROUTE].rearrange("p (t g) -> p t g", t=TT)))
                gl = lg[:, :, 0:N_GROUPS]
                el = lg[:, :, N_GROUPS:]

                def quad(i):
                    return rt[:, i, :, 0:4]

                def col(i):
                    return small[:, i, :]

                def first_max(values, best, pick, tmp, idx):
                    then(dve.tensor_reduce(col(best), values, AX.X, ALU.max))
                    then(dve.tensor_tensor(tmp, values, col(best).unsqueeze(2).broadcast_to([P, TT, 4]), ALU.is_equal))
                    then(dve.scalar_tensor_tensor(tmp, tmp, -8.0, iota_e[:, :, :], ALU.mult, ALU.add))
                    then(dve.tensor_reduce(col(idx), tmp, AX.X, ALU.min))
                    then(dve.tensor_scalar(col(idx), col(idx), 8.0, None, ALU.add))
                    then(dve.tensor_tensor(pick, iota_e[:, :, :], col(idx).unsqueeze(2).broadcast_to([P, TT, 4]),
                                           ALU.is_equal))

                first_max(gl, 14, quad(0), quad(1), 15)
                ex_in = small[:, 0:4, :].rearrange("p g t -> p t g")
                then(dve.tensor_tensor(ex_in, gl, col(14).unsqueeze(2).broadcast_to([P, TT, 4]), ALU.subtract))
                chosen = rt[:, 2, :, :].rearrange("p t (g e) -> p t g e", g=N_GROUPS)
                then(dve.tensor_tensor(chosen, el.rearrange("p t (g e) -> p t g e", g=N_GROUPS),
                                       quad(0).unsqueeze(3).broadcast_to([P, TT, N_GROUPS, PER_GROUP]), ALU.mult))
                then(dve.tensor_reduce(quad(3), chosen.rearrange("p t g e -> p t e g"), AX.X, ALU.add))
                first_max(quad(3), 16, quad(4), quad(5), 17)
                then(dve.scalar_tensor_tensor(quad(6), quad(4), -FAR, quad(3), ALU.mult, ALU.add))
                first_max(quad(6), 18, quad(7), quad(5), 19)
                dve.tensor_tensor(col(4), col(18), col(16), ALU.subtract).then_inc(exp_in_ready, 1)
                group = quad(0).unsqueeze(3).broadcast_to([P, TT, N_GROUPS, PER_GROUP])
                then(dve.tensor_tensor(quad(9), quad(4), quad(7), ALU.add))
                then(dve.tensor_tensor(quad(9), quad(9), fresh[:, :].unsqueeze(2).broadcast_to([P, TT, 4]), ALU.mult))
                dve.tensor_tensor(sel[:, :, :].rearrange("p t (g e) -> p t g e", g=N_GROUPS), group,
                                  quad(9).unsqueeze(2).broadcast_to([P, TT, N_GROUPS, PER_GROUP]), ALU.mult)\
                   .then_inc(sel_ready, 1)
                dve.wait_ge(exp_ready, l + 1)
                then(dve.tensor_reduce(col(20), small[:, 8:12, :].rearrange("p g t -> p t g"), AX.X, ALU.add))
                then(dve.tensor_scalar(col(21), col(12), 1.0, None, ALU.add))
                then(dve.tensor_tensor(col(20), col(20), col(21), ALU.mult))
                then(dve.reciprocal(col(22), col(20)))
                then(dve.tensor_tensor(col(23), col(22), col(12), ALU.mult))
                then(dve.tensor_tensor(quad(8), quad(4), col(22).unsqueeze(2).broadcast_to([P, TT, 4]), ALU.mult))
                then(dve.tensor_tensor(quad(9), quad(7), col(23).unsqueeze(2).broadcast_to([P, TT, 4]), ALU.mult))
                then(dve.tensor_tensor(quad(8), quad(8), quad(9), ALU.add))
                then(dve.tensor_tensor(gate_n[:, :, :].rearrange("p t (g e) -> p t g e", g=N_GROUPS), group,
                                       quad(8).unsqueeze(2).broadcast_to([P, TT, N_GROUPS, PER_GROUP]), ALU.mult))
                dve.wait_ge(pos_ps, l + 1)
                dve.scalar_tensor_tensor(pos1[:, :, :], misc[:, 0:TT * EXPERTS].rearrange("p (t e) -> p t e", t=TT),
                                         1.0, sel[:, :, :], ALU.add, ALU.mult).then_inc(pos_ready, 1)
                then(dve.tensor_reduce(busiest[:, :], misc[:, TT * EXPERTS:(TT + 1) * EXPERTS], AX.X, ALU.max))
                then(dve.tensor_tensor(needed[:, :], limits[:, :], busiest[:, :].broadcast_to([P, ROUNDS]), ALU.is_lt))
                then(dve.tensor_reduce(rounds_n[:, :], needed[:, :], AX.X, ALU.add))
                then(dve.tensor_tensor(rounds_f[:, :], rounds_f[:, :], rounds_n[:, :], ALU.add))
                dve.tensor_scalar(rounds_at[:, bass.ds(l + 1, 1)], rounds_f[:, :], 1.0, None, ALU.mult)\
                   .then_inc(rounds_ready, 1)
                dve.wait_ge(rounds_ready, OPEN + l + 1)
                for i, bank in enumerate(wide):
                    dve.wait_ge(xn_hi_ready, l * 2 * TT + i + 1)
                    cols = slice(i % 2 * 512, (i % 2 + 1) * 512)
                    dve.tensor_tensor(xn_lo[:, i // 2, cols], bank, xn_hi[:, i // 2, cols], ALU.subtract)\
                       .then_inc(xn_lo_ready, 1)
                r.end()

                last = rounds_before(dve, l + 1)
                fill_slots(l, first * QUADS, 0)
                with dve.Fori(first, last) as rd:
                    with dve.Fori(0, QUADS) as q:
                        qd = rd * QUADS + q
                        dve.wait_ge(slots_ps, qd + 1)
                        for e in range(2):
                            rows = slice(e * SLOTS, (e + 1) * SLOTS)
                            dve.tensor_copy(slot_gate[rows, :],
                                            misc[rows, 0:4].rearrange("p (a e) -> p a e", e=2)[:, :, e])\
                               .then_inc(slot_gate_ready, 1)
                        dve.tensor_copy(back[:, :, :],
                                        misc_h[:, BACK_AT:BACK_AT + 2 * T].rearrange("p (a t) -> p a t", a=2))\
                           .then_inc(back_ready, 1)
                        dve.wait_ge(slot_gate_ready, (qd + 1) * 2)
                        for p in range(2):
                            pr = qd * 2 + p
                            dve.wait_ge(sg_ready, pr + 1)
                            dve.tensor_tensor(sg[:, p, :], acc[p][:, 0:D_EXPERT], sg[:, p, :], ALU.mult)\
                               .then_inc(silu_ready, 1)
                            dve.wait_ge(silu_ready, pr + 1)
                            dve.scalar_tensor_tensor(hid[:, p, :], acc[p][:, D_EXPERT:], slot_gate[:, p:p + 1],
                                                     sg[:, p, :], ALU.mult, ALU.mult).then_inc(hid_ready, 1)
                        with dve.If(qd + 1 < last * QUADS):
                            fill_slots(l, qd + 1, (q + 1) % QUADS)
                        for p in range(2):
                            for dh in range(2):
                                cols = slice(dh * 512, (dh + 1) * 512)
                                dve.wait_ge(ys_hi_ready, qd * 4 + p * 2 + dh + 1)
                                dve.tensor_tensor(ys_lo[:, p, cols], y_ps(p, dh), ys_hi[:, p, cols], ALU.subtract)\
                                   .then_inc(ys_lo_ready, 1)
                        dve.wait_ge(h_added, OPEN + qd * KT)
                        for m in range(KT):
                            dve.wait_ge(combined, OPEN + qd * KT + m + 1)
                            dve.tensor_tensor(h_t[:, m, :], num[:, (m + 2) % 3, 0:T], h_t[:, m, :], ALU.add)\
                               .then_inc(h_added, 1)
            norm(2 * DEPTH, fin_gain)

        @block.tensor
        def _(pe):
            pe.wait_ge(consts, N_CONST)
            pe.wait_ge(padded, 10 + 4)

            def mean_square(i):
                for k in range(KT):
                    pe.wait_ge(sq_ready, i * KT + k + 1)
                    mm = pe.matmul(misc[:, 0:T], ones[:, :], norm_buf[:, k, :], start=(k == 0), stop=(k == KT - 1))
                mm.then_inc(ms_ready, 1)

            def three(dst, hi, lo, rhi, rlo, first, last):
                pe.matmul(dst, hi, rhi, start=first, stop=False)
                pe.matmul(dst, hi, rlo, start=False, stop=False)
                return pe.matmul(dst, lo, rhi, start=False, stop=last)

            def dense(l, n, slot, bank, rhi, rlo):
                pe.wait_ge(lo_done, RING + l * DENSE + n + 1)
                for k in range(KT):
                    cols = slice(k * P, (k + 1) * P)
                    mm = three(acc[bank][:, 0:T], w_hi[:, slot, cols], w_lo[:, slot, cols], rhi[:, k, :], rlo[:, k, :],
                               k == 0, k == KT - 1)
                mm.then_inc(tiles_done, 1)

            def gather(qd, side):
                if side == 0:
                    pe.wait_ge(pick_ready_q, qd + 1)
                for k in range(side * KT // 2, (side + 1) * KT // 2):
                    bank = [b_s, b_t][k // 2 % 2]
                    if k % 2 == 0 and k >= 4:
                        pe.wait_ge(xg_ready, qd * KP + k // 2 - 1)
                    for t in range(TT):
                        for part in (xn_hi, xn_lo):
                            mm = pe.matmul(bank[:, k % 2 * 4 * SLOTS:(k % 2 + 1) * 4 * SLOTS],
                                           part[:, t, k * P:(k + 1) * P], pick[:, t, :],
                                           start=(t == 0 and part is xn_hi), stop=(t == TT - 1 and part is xn_lo),
                                           skip_group_check=True)
                    if k % 2:
                        mm.then_inc(gathered, 1)

            def turn_slots(qd):
                pe.wait_ge(gate_q_ready, (qd + 1) * 2)
                pe.wait_ge(back_ready, OPEN + qd)
                for p in range(2):
                    cols = slice(p * 2 * SLOTS, (p + 1) * 2 * SLOTS)
                    for t in range(TT):
                        for part in range(2):
                            pe.matmul(misc[:, 2 * p:2 * p + 2], pick[:, t, cols], gate_q[:, part, t, 2 * p:2 * p + 2],
                                      start=(t == 0 and part == 0), stop=(t == TT - 1 and part == 1),
                                      skip_group_check=True)
                for p in range(2):
                    cols = slice(p * 2 * SLOTS, (p + 1) * 2 * SLOTS)
                    for t in reversed(range(TT)):
                        at = BACK_AT + p * T + R_START[t]
                        mm = pe.transpose(misc_h[:, at:at + P], pick[:, t, cols], ident_h[:, :])
                mm.then_inc(slots_ps, 1)

            def turn_hid(qd, p):
                pe.wait_ge(hid_ready, qd * 2 + p + 1)
                for f in range(FT):
                    mm = pe.transpose(num[:, 2, (p * FT + f) * P:(p * FT + f + 1) * P], hid[:, p, f * P:(f + 1) * P],
                                      ident[:, :])
                mm.then_inc(hid_turned, 1)

            def down(qd, p):
                pe.wait_ge(hid_t_ready, qd * 2 + p + 1)
                for f in range(FT):
                    for e in range(2):
                        pe.wait_ge(down_landed[p][f * 2 + e], (qd + 1) * 16)
                    for dh in range(2):
                        for e in range(2):
                            rows = slice(e * SLOTS, (e + 1) * SLOTS)
                            mm = pe.matmul(y_ps(p, dh)[rows, :], hid_t[:, p, f, rows],
                                           down_slot(p, f * 2 + e)[:, dh * 512:(dh + 1) * 512],
                                           start=(f == 0), stop=(f == FT - 1), skip_group_check=True)
                    mm.then_inc(down_done, 1)

            with pe.Fori(0, DEPTH) as l:
                first = rounds_before(pe, l)
                mean_square(l * 2)
                pe.wait_ge(prep_done, (l + 1) * PREP)
                pe.wait_ge(std_ready, l * 2 + 1)
                for k in range(KT):
                    pe.wait_ge(x_lo_ready, l * KT + k + 1)
                    mm = three(misc[0:GROWS, 0:T], gate_hi[:, k, :], gate_lo[:, k, :], x_hi[:, k, :], x_lo[:, k, :],
                               k == 0, k == KT - 1)
                mm.then_inc(gates_ready, 1)
                pe.wait_ge(floor_ready, l + 1)
                for t in range(TT):
                    mm = pe.transpose(misc[:, t * P:(t + 1) * P], a_floor[:, t * P:(t + 1) * P], ident[:, :])
                mm.then_inc(a_col_ps, 1)
                for h in range(HEADS):
                    bank = [b_s, b_t][h % 2]
                    pe.wait_ge(pick_ready, (l + 1) * HEADS)
                    if h >= 2:
                        pe.wait_ge(decay_ready, (l * HEADS + h - 1) * TT)
                    pe.matmul(bank[:, 0:CAUSAL], ones[0:HEADS, :], g_pick[:, h, :], start=True, stop=False)
                    pe.matmul(bank[:, 0:CAUSAL], ident_b[:, :], ahead[:, :], start=False, stop=True)\
                      .then_inc(arg_ready, 1)
                with pe.Fori(0, HEADS) as h:
                    hd = l * HEADS + h
                    for i in range(PER_HEAD):
                        prev = (i - 2) % PER_HEAD
                        if i < 2:
                            pe.wait_ge(sig_c_ready, OPEN + hd * 2)
                        elif prev < GM0:
                            pe.wait_ge(qkv_ready, hd * 4 + prev + 1)
                        else:
                            read = {GM0: sig_m_ready, CX0: cx_ready, CC0: cc_read, CB0: cb_read}[prev - prev % 2]
                            pe.wait_ge(read, hd * 2 + prev % 2 + 1)
                        dense(l, h * PER_HEAD + i, i % RING, i % 2, x_hi, x_lo)
                        if i == GM0:
                            pe.wait_ge(qkv_ready, hd * 4 + 4)
                            pe.wait_ge(hm_ready, OPEN + hd * TT)
                            for t in range(TT):
                                for v in range(2):
                                    mm = pe.transpose(num[:, t, v * P:(v + 1) * P], v_t[:, v, t * P:(t + 1) * P],
                                                      ident[:, :])
                            mm.then_inc(v_turned, 1)
                            pe.wait_ge(ym_ready, OPEN + hd * 2)
                            pe.wait_ge(decay_ready, (l + 1) * HEADS * TT)
                            for s in range(TT):
                                mm = pe.matmul(b_s[:, CAUSAL_AT[s]:CAUSAL_AT[s] + CAUSAL_W[s]],
                                               k_t[:, s * P:(s + 1) * P], q_t[:, T_START[s]:T],
                                               start=(s == 0), stop=(s == TT - 1), skip_group_check=True)
                            mm.then_inc(scores_ready, 1)
                        if i == CX0 + 1:
                            pe.wait_ge(s_w_ready, (hd + 1) * TT)
                            pe.wait_ge(v_n_ready, hd + 1)
                            for t in range(TT):
                                for s in range(t + 1):
                                    mm = pe.matmul(num[:, t, 0:DV + 1], s_w[0:T_SIZE[s], s, t * P:(t + 1) * P],
                                                   v_n[0:T_SIZE[s], s, :], start=(s == 0), stop=(s == t))
                            mm.then_inc(num_ready, 1)
                        if i == CB0 + 1:
                            pe.wait_ge(hm_ready, OPEN + (hd + 1) * TT)
                            for v, bank in enumerate((b_s, b_t)):
                                for t in range(TT):
                                    mm = pe.transpose(bank[:, t * P:t * P + T_SIZE[t]],
                                                      hm[0:T_SIZE[t], t, v * P:(v + 1) * P],
                                                      ident[0:T_SIZE[t], 0:T_SIZE[t]])
                            mm.then_inc(hm_turned, 1)

                pe.wait_ge(y_ready, OPEN + (l + 1) * HEADS)
                for m in range(KT):
                    n = HEADS * PER_HEAD + m
                    if m < 2:
                        pe.wait_ge(sig_c_ready, OPEN + (l + 1) * HEADS * 2)
                    else:
                        pe.wait_ge(h_mixed, l * KT + m - 1)
                    dense(l, n, n % RING, n % 2, y_hi, y_lo)

                mean_square(l * 2 + 1)
                pe.wait_ge(std_ready, l * 2 + 2)
                for t in range(TT):
                    dst = misc[:, t * N_ROUTE:(t + 1) * N_ROUTE]
                    pe.matmul(dst, ones[0:1, :], prm[0:1, C_BROUTE:C_ALL], start=(t == 0), stop=False,
                              skip_group_check=True)
                    for k in range(KT):
                        if t == 0:
                            pe.wait_ge(x_ready, (l * 2 + 1) * KT + k + 1)
                        mm = pe.matmul(dst, norm_buf[:, k, R_START[t]:R_START[t] + P],
                                       prm[:, C_ROUTE + k * N_ROUTE:C_ROUTE + (k + 1) * N_ROUTE],
                                       start=False, stop=(k == KT - 1), skip_group_check=True)
                mm.then_inc(logits_ready, 1)
                for i, bank in enumerate(wide):
                    for j in range(4):
                        mm = pe.transpose(bank[:, j * P:(j + 1) * P],
                                          norm_buf[:, i % 2 * 4 + j, R_START[i // 2]:R_START[i // 2] + P], ident[:, :])
                    mm.then_inc(xn_turned, 1)
                pe.wait_ge(sel_ready, l + 1)
                for t in range(TT):
                    for s in range(t + 1):
                        mm = pe.matmul(misc[:, t * EXPERTS:(t + 1) * EXPERTS], (before if s == t else one_h)[:, :],
                                       sel[:, s, :], start=(s == 0), stop=(s == t))
                for s in range(TT):
                    mm = pe.matmul(misc[:, TT * EXPERTS:(TT + 1) * EXPERTS], one_h[:, :], sel[:, s, :],
                                   start=(s == 0), stop=(s == TT - 1))
                mm.then_inc(pos_ps, 1)

                last = rounds_before(pe, l + 1)
                pe.wait_ge(xn_lo_ready, (l + 1) * 2 * TT)
                gather(first * QUADS, 0)
                gather(first * QUADS, 1)
                turn_slots(first * QUADS)
                with pe.Fori(first, last) as rd, pe.Fori(0, QUADS) as q:
                    qd = rd * QUADS + q
                    pe.wait_ge(xg_ready, (qd + 1) * KP)
                    pe.wait_ge(ys_lo_ready, OPEN + qd * 4)
                    for p in range(2):
                        for kp in range(KP):
                            if p == 1 and kp == 2:
                                pe.wait_ge(h_added, OPEN + qd * KT)
                                turn_hid(qd, 0)
                            for e in range(2):
                                pe.wait_ge(gu_landed[p][kp * 2 + e], (qd + 1) * 16)
                            for k in (2 * kp, 2 * kp + 1):
                                for e in range(2):
                                    at = (p * 2 + e) * SLOTS
                                    mm = pe.matmul(acc[p][e * SLOTS:(e + 1) * SLOTS, :], xg[:, k, at:at + SLOTS],
                                                   gu_slot(p, kp * 2 + e)[:, k % 2 * 512:(k % 2 + 1) * 512],
                                                   start=(k == 0), stop=(k == KT - 1))
                            mm.then_inc(gu_done, 1)
                    down(qd, 0)
                    turn_hid(qd, 1)
                    with pe.If(qd + 1 < last * QUADS):
                        gather(qd + 1, 0)
                    down(qd, 1)
                    with pe.If(qd + 1 < last * QUADS):
                        gather(qd + 1, 1)
                        turn_slots(qd + 1)
                    pe.wait_ge(back_ready, OPEN + qd + 1)
                    pe.wait_ge(ys_lo_ready, OPEN + (qd + 1) * 4)
                    for m in range(KT):
                        if m >= 3:
                            pe.wait_ge(h_added, OPEN + qd * KT + m - 2)
                        for p in range(2):
                            for part in (ys_hi, ys_lo):
                                mm = pe.matmul(num[:, (m + 2) % 3, 0:T], part[:, p, m * P:(m + 1) * P],
                                               back[:, p, :], start=(p == 0 and part is ys_hi),
                                               stop=(p == 1 and part is ys_lo))
                        mm.then_inc(combined, 1)
            mean_square(2 * DEPTH)


def lay_out(x, meta_tokens, norm_mix, w_in, b_if, conv_w, mh_gain, w_out, norm_ffn,
            w_group, b_group, w_router, b_router, w_gate, w_up, w_down, norm_final):
    import numpy as np

    def columns(v):
        return np.moveaxis(v.reshape(*v.shape[:-1], -1, P), -1, -2)

    h_in = columns(np.moveaxis(np.concatenate([meta_tokens, x[0]], axis=0), 0, 0))
    h_in = np.transpose(h_in, (1, 2, 0))

    def tiles(w):
        w = w.reshape(DEPTH, KT, P, -1, P)
        return np.transpose(w, (0, 3, 2, 1, 4))

    qk, vw = HEADS * P, D
    at = np.cumsum([0, qk, qk, vw, HEADS, HEADS, vw, D, D, D, D])
    q, k, v, ig, fg, gm, cx, cb, cc, gc = (w_in[:, :, a:b] for a, b in zip(at[:-1], at[1:]))
    q, k, v, gm, cx, cb, cc, gc, wo = (tiles(a) for a in (q, k, v, gm, cx, cb, cc, gc, w_out))
    order = []
    for h in range(HEADS):
        two = slice(2 * h, 2 * h + 2)
        order += [q[:, h:h + 1], k[:, h:h + 1], v[:, two], gm[:, two], cx[:, two], cc[:, two], cb[:, two], gc[:, two]]
    dense_w = np.concatenate([*order, wo], axis=1).reshape(DEPTH, DENSE, P, D)

    gate_up = np.concatenate([w_gate, w_up], axis=3)
    gate_up = gate_up.reshape(DEPTH, PAIRS, 2, KP, 2, P, 2 * D_EXPERT)
    gate_up = np.transpose(gate_up, (0, 1, 3, 2, 5, 4, 6)).reshape(DEPTH, PAIRS, GU_TILES, P, D)
    down = w_down.reshape(DEPTH, PAIRS, 2, FT, P, D)
    down = np.transpose(down, (0, 1, 3, 2, 4, 5)).reshape(DEPTH, PAIRS, 2 * FT, P, D)
    moe_w = np.concatenate([gate_up, down], axis=2).reshape(DEPTH, MOE, P, D)

    def rows(w):
        return np.transpose(w.reshape(DEPTH, KT, P, -1), (0, 2, 1, 3)).reshape(DEPTH, P, -1)

    b_gates = np.zeros((DEPTH, P, 1), np.float32)
    b_gates[:, 0:HEADS, 0] = b_if[:, :HEADS]
    b_gates[:, F_ROW:GROWS, 0] = b_if[:, HEADS:]
    b_route = np.zeros((DEPTH, P, N_ROUTE), np.float32)
    b_route[:, 0, :N_GROUPS] = b_group
    b_route[:, 0, N_GROUPS:] = b_router
    conv = np.transpose(columns(conv_w), (0, 2, 1, 3)).reshape(DEPTH, P, -1)
    params = np.concatenate([columns(norm_mix), columns(norm_ffn), columns(mh_gain), conv,
                             rows(np.concatenate([ig, fg], axis=2)),
                             rows(np.concatenate([w_group, w_router], axis=2)), b_gates, b_route], axis=2)
    params = np.transpose(params, (1, 0, 2))
    return {"h_in": h_in, "params": params, "norm_final": columns(norm_final), "dense_w": dense_w, "moe_w": moe_w}


def kernel(**inputs):
    import numpy as _np
    import concourse.bacc as _bacc
    from concourse.bass_utils import run_bass_kernel_spmd as _run

    nc = _bacc.Bacc("TRN2", target_bir_lowering=False, num_devices=1)
    arrays = {name: _np.ascontiguousarray(a) for name, a in
              lay_out(**{name: _np.asarray(a) for name, a in inputs.items()}).items()}
    args = [nc.dram_tensor(name, a.shape, F32, kind="ExternalInput").ap() for name, a in arrays.items()]
    args.append(nc.dram_tensor("out_t", (P, KT, SEQ), F32, kind="ExternalOutput").ap())
    build(nc, *args)
    r = _run(nc, [arrays], core_ids=[0])
    got = r.results[0]["out_t"]
    return _np.ascontiguousarray(_np.transpose(got, (2, 1, 0)).reshape(1, SEQ, D))
```

```python
from contextlib import ExitStack

import concourse.bass as bass
from concourse import mybir

F32 = mybir.dt.float32
F16 = mybir.dt.float16
BF16 = mybir.dt.bfloat16
ALU = mybir.AluOpType
ACT = mybir.ActivationFunctionType
AX = mybir.AxisListType

P = 128
DEPTH = 2
D = 1024
KT = D // P
N_META = 16
SEQ = 256
T = N_META + SEQ
HEADS = 4
DV = D // HEADS
EPS = 1e-6
CONV_K = 3
N_GROUPS, PER_GROUP = 4, 4
EXPERTS = N_GROUPS * PER_GROUP
D_EXPERT = 256
FT = D_EXPERT // P
W_SCALE = 64.0
UNSCALE = 1.0 / W_SCALE
FAR = 1e30

TT = 3
TP = TT * P
T_START = [0, P, 2 * P]
T_SIZE = [P, P, T - 2 * P]
R_START = [0, P, T - P]
NEW_ROWS = slice(P - 32, P)
LOW_ROWS = slice(P - 64, P - 32)
assert T_SIZE[TT - 1] <= 32
CAUSAL_AT = [0, T, T + (T - P)]
CAUSAL_W = [T, T - P, T - 2 * P]
CAUSAL = sum(CAUSAL_W)

Q, K, V0, GM0, CX0, CC0, CB0, GC0, PER_HEAD = 0, 1, 2, 4, 6, 8, 10, 12, 14
DENSE = HEADS * PER_HEAD + KT
RING = 7
SLOTS = 64
PAIRS = EXPERTS // 2
QUADS = EXPERTS // 4
H_PARTS = 4
ROUNDS = (T + SLOTS - 1) // SLOTS
KP = KT // 2
GU_TILES = 2 * KP
PER_PAIR = GU_TILES + 2 * FT
MOE = PAIRS * PER_PAIR

C_MIX = 0
C_FFN = C_MIX + KT
C_GAIN = C_FFN + KT
C_CONV = C_GAIN + KT
C_GATE = C_CONV + CONV_K * KT
C_ROUTE = C_GATE + KT * 2 * HEADS
N_ROUTE = N_GROUPS + EXPERTS
C_BIF = C_ROUTE + KT * N_ROUTE
C_BROUTE = C_BIF + 1
C_ALL = C_BROUTE + N_ROUTE
F_ROW = 32
GROWS = F_ROW + HEADS

OPEN = 1


class Chain:

    def __init__(self, eng, sem, base, total):
        self.eng, self.sem, self.base, self.total, self.n = eng, sem, base, total, 0

    def step(self, ins):
        ins.then_inc(self.sem, 1)
        self.n += 1

    def settle(self):
        self.eng.wait_ge(self.sem, self.base + self.n)

    def end(self):
        assert self.n == self.total, (self.sem, self.n, self.total)


def ring_use(l, use, slot):
    return l * ((DENSE - slot + RING - 1) // RING) + use


def build(nc, h_in, params, norm_final, dense_w, moe_w, out):
    with ExitStack() as ctx:
        def sb(name, shape, dt=F32):
            return ctx.enter_context(nc.sbuf_tensor(name, shape, dt))

        def pb(name, shape, dt=F32):
            return ctx.enter_context(nc.psum_tensor(name, shape, dt))

        def sem(name):
            return ctx.enter_context(nc.semaphore(name))

        h_t = sb("h_t", [P, KT, T])
        norm_buf = sb("norm_buf", [P, KT, T])
        x_parts = sb("x_parts", [P, 2, KT, T], F16)
        x_hi, x_lo = x_parts[:, 0, :, :], x_parts[:, 1, :, :]
        y_hi = sb("y_hi", [P, KT, T], F16)
        y_lo = sb("y_lo", [P, KT, T], F16)
        raw = sb("raw", [P, RING, D])
        w_hi = sb("w_hi", [P, RING, D], F16)
        w_lo = sb("w_lo", [P, RING, D], F16)
        m_raw = sb("m_raw", [P, 2 * GU_TILES + 2 * FT, D])
        prm_all = sb("prm_all", [P, DEPTH, C_ALL])
        prm = sb("prm", [P, C_ALL])
        fin_gain = sb("fin_gain", [P, KT])
        gate_hi = sb("gate_hi", [P, KT, GROWS], F16)
        gate_lo = sb("gate_lo", [P, KT, GROWS], F16)
        ones = sb("ones", [P, P])
        ident = sb("ident", [P, P])
        ident_b = sb("ident_b", [P, P], BF16)
        ahead = sb("ahead", [P, CAUSAL], BF16)
        eps = sb("eps", [P, 1])
        mean = sb("mean", [P, P])
        half = sb("half", [P, TT])
        a_floor = sb("a_floor", [P, TP])
        a_col = sb("a_col", [P, TT, GROWS])
        scratch = sb("scratch", [P, HEADS * CAUSAL])
        cx, cv, ym = (scratch[:, i * 2 * T:(i + 1) * 2 * T].rearrange("p (a t) -> p a t", a=2) for i in range(3))
        g_pick = scratch[0:HEADS, :].rearrange("p (h c) -> p h c", h=HEADS)
        norm_flat = norm_buf[:, :, :].rearrange("p k t -> p (k t)")
        decay = norm_flat[:, 0:HEADS * CAUSAL].rearrange("p (h c) -> p h c", h=HEADS)
        squared = norm_flat[:, 0:TT * 512].bitcast(BF16).rearrange("p (i c) -> p i c", i=2 * TT)
        q_t = norm_flat[:, HEADS * CAUSAL:HEADS * CAUSAL + T]
        k_t = sb("k_t", [P, TP])
        v_flat = sb("v_flat", [P, TT * DV])
        v_t = v_flat[:, :].rearrange("p (v t) -> p v t", v=2)
        rstd = v_flat[:, T:2 * T]
        hm = v_flat[:, :].rearrange("p (t d) -> p t d", t=TT)
        v_n = sb("v_n", [P, TT, DV + 1])
        s_w = sb("s_w", [P, TT, TP])
        sig_m = sb("sig_m", [P, 2, T])
        sig_c = sb("sig_c", [P, 2, T])
        i_gate, f_sum, g_max, m_row = (b[0:HEADS, j, :] for b in (sig_m, sig_c) for j in range(2))
        f_gate, f_abs, f_exp, f_log = (b[F_ROW:GROWS, j, :] for b in (sig_m, sig_c) for j in range(2))
        u = sb("u", [P, 2, T + CONV_K - 1])
        ssq = sb("ssq", [P, TT])
        den = sb("den", [P, TT])
        stat = sb("stat", [P, 6, TT])
        route_w = sb("route_w", [P, KT, N_ROUTE])
        ms_tok = sb("ms_tok", [P, 2, TT])
        rstd_tok = sb("rstd_tok", [P, TT])
        down_count = sb("down_count", [P, EXPERTS])
        lg = sb("lg", [P, TT, N_ROUTE])
        small = sb("small", [P, 24, TT])
        gate_n = sb("gate_n", [P, TT, EXPERTS])
        sel = sb("sel", [P, TT, EXPERTS], F16)
        pos1 = sb("pos1", [P, TT, EXPERTS])
        place = sb("place", [P, SLOTS])
        before = sb("before", [P, P], F16)
        one_h = sb("one_h", [P, P], F16)
        ident_h = sb("ident_h", [P, P], F16)
        limits = sb("limits", [P, ROUNDS])
        busiest = sb("busiest", [P, 1])
        needed = sb("needed", [P, ROUNDS])
        rounds_n = sb("rounds_n", [P, 1])
        rounds_f = sb("rounds_f", [P, 1])
        opened = sb("opened", [1, 16])
        rounds_at = sb("rounds_at", [P, DEPTH + 1], mybir.dt.int32)
        fresh = sb("fresh", [P, TT])
        gate_q = sb("gate_q", [P, 2, TT, 4], F16)
        slot_gate = sb("slot_gate", [P, 2])
        xn_hi = w_hi[:, RING - TT:, :]
        xn_lo = w_lo[:, RING - TT:, :]

        def gu_slot(p, i):
            return m_raw[:, p * GU_TILES + i, :]

        def down_slot(p, i):
            return m_raw[:, 2 * GU_TILES + i, :] if p == 0 else raw[:, i, :]

        xg = x_parts[:, :, :, :].rearrange("p a k t -> p (a k t)").bitcast(F32)[:, 0:KT * 4 * SLOTS]\
            .rearrange("p (k s) -> p k s", k=KT)
        sg = sig_m[:, :, :].rearrange("p a t -> p (a t)")[:, 0:2 * D_EXPERT].rearrange("p (a f) -> p a f", a=2)
        hid = sig_c[:, :, :].rearrange("p a t -> p (a t)")[:, 0:2 * D_EXPERT].rearrange("p (a f) -> p a f", a=2)
        hid_hi, hid_lo = (scratch[:, i * FT * P:(i + 1) * FT * P].bitcast(F16)
                          .rearrange("p (a f s) -> p a f s", a=2, f=FT) for i in range(2))
        DOWN = 2 * FT
        down_hi = [w_hi[:, 0:DOWN, :], norm_flat[:, 0:DOWN * D // 2].bitcast(F16).rearrange("p (i d) -> p i d", i=DOWN)]
        down_lo = [w_lo[:, 0:DOWN, :], raw[:, DOWN:RING - 1, :].rearrange("p i d -> p (i d)").bitcast(F16)
                   .rearrange("p (i d) -> p i d", i=DOWN)]
        RT_AT = 2 * FT * P
        PICK_AT = RT_AT + 7 * TT * N_ROUTE
        rt = scratch[:, RT_AT:PICK_AT].rearrange("p (i t e) -> p i t e", i=7, t=TT)
        pick = scratch[:, PICK_AT:PICK_AT + TT * 2 * SLOTS].bitcast(F16).rearrange("p (t s) -> p t s", t=TT)
        back = v_flat[:, 0:T].bitcast(F16).rearrange("p (a t) -> p a t", a=2)
        ys_hi = y_hi[:, :, :].rearrange("p k t -> p (k t)")[:, 0:2 * D].rearrange("p (a d) -> p a d", a=2)
        ys_lo = y_lo[:, :, :].rearrange("p k t -> p (k t)")[:, 0:2 * D].rearrange("p (a d) -> p a d", a=2)

        acc = [pb(f"acc{i}", [P, 512]) for i in range(2)]
        b_s = pb("b_s", [P, 512])
        b_t = pb("b_t", [P, 512])
        num = pb("num", [P, TT, 512])
        misc = pb("misc", [P, 512])
        misc_h = misc[:, :].bitcast(F16)
        BACK_AT = 64

        h_loaded = [sem(f"h_loaded{i}") for i in range(H_PARTS)]
        prm_loaded = sem("prm_loaded")
        consts = sem("consts")
        zeroed = sem("zeroed")
        padded = sem("padded")
        raw_landed = [sem(f"raw_landed{i}") for i in range(RING)]
        hi_done = sem("hi_done")
        lo_done = sem("lo_done")
        tiles_done = sem("tiles_done")
        gu_landed = [[sem(f"gu_landed{p}_{i}") for i in range(GU_TILES)] for p in range(2)]
        down_landed = [[sem(f"down_landed{p}_{i}") for i in range(2 * FT)] for p in range(2)]
        gu_done = sem("gu_done")
        down_done = sem("down_done")
        down_hi_ready = sem("down_hi_ready")
        down_split = sem("down_split")
        prep_done = sem("prep_done")
        sq_ready = sem("sq_ready")
        ms_ready = sem("ms_ready")
        ln_ready = sem("ln_ready")
        ms_tok_ready = sem("ms_tok_ready")
        ms_tok_summed = sem("ms_tok_summed")
        rstd_tok_ready = sem("rstd_tok_ready")
        rstd_ready = sem("rstd_ready")
        x_ready = sem("x_ready")
        x_hi_ready = sem("x_hi_ready")
        x_lo_ready = sem("x_lo_ready")
        gates_ready = sem("gates_ready")
        gate_step = sem("gate_step")
        pick_step = sem("pick_step")
        f_abs_ready = sem("f_abs_ready")
        f_exp_ready = sem("f_exp_ready")
        f_log_ready = sem("f_log_ready")
        m_row_ready = sem("m_row_ready")
        floor_ready = sem("floor_ready")
        pick_ready = sem("pick_ready")
        a_col_ps = sem("a_col_ps")
        a_col_ready = sem("a_col_ready")
        arg_ready = sem("arg_ready")
        decay_ready = sem("decay_ready")
        qkv_ready = sem("qkv_ready")
        v_turned = sem("v_turned")
        v_n_ready = sem("v_n_ready")
        scores_ready = sem("scores_ready")
        s_w_ready = sem("s_w_ready")
        num_ready = sem("num_ready")
        ssq_ready = sem("ssq_ready")
        head_step = sem("head_step")
        var_ready = sem("var_ready")
        pow_ready = sem("pow_ready")
        f_ready = sem("f_ready")
        hm_ready = sem("hm_ready")
        hm_turned = sem("hm_turned")
        sig_m_ready = sem("sig_m_ready")
        sig_c_ready = sem("sig_c_ready")
        cx_ready = sem("cx_ready")
        y_ready = sem("y_ready")
        ym_ready = sem("ym_ready")
        cc_read = sem("cc_read")
        cb_read = sem("cb_read")
        h_mixed = sem("h_mixed")
        logits_ready = sem("logits_ready")
        route_step = sem("route_step")
        exp_in_ready = sem("exp_in_ready")
        exp_ready = sem("exp_ready")
        h_turned = sem("h_turned")
        xn_hi_ready = sem("xn_hi_ready")
        xn_lo_ready = sem("xn_lo_ready")
        sel_ready = sem("sel_ready")
        pos_ps = sem("pos_ps")
        pos_ready = sem("pos_ready")
        rounds_ready = sem("rounds_ready")
        gate_q_ready = sem("gate_q_ready")
        picked = sem("picked")
        pick_ready_q = sem("pick_ready_q")
        gathered = sem("gathered")
        xg_ready = sem("xg_ready")
        slots_ps = sem("slots_ps")
        slot_gate_ready = sem("slot_gate_ready")
        back_ready = sem("back_ready")
        sg_ready = sem("sg_ready")
        silu_ready = sem("silu_ready")
        hid_ready = sem("hid_ready")
        hid_turned = sem("hid_turned")
        hid_hi_ready = sem("hid_hi_ready")
        hid_lo_ready = sem("hid_lo_ready")
        ys_hi_ready = sem("ys_hi_ready")
        ys_lo_ready = sem("ys_lo_ready")
        combined = sem("combined")
        h_added = sem("h_added")
        out_stored = sem("out_stored")

        wide = [[num[:, 0, :], num[:, 1, :], num[:, 2, :]], [b_s[:, :], b_t[:, :], acc[0][:, :]]]

        def y_ps(p, dh):
            return num[:, dh, :] if p == 0 else acc[dh][:, :]

        def rounds_before(eng, l):
            if eng is not nc.vector:
                eng.wait_ge(rounds_ready, OPEN + l)
            return eng.value_load(rounds_at[0:1, bass.ds(l, 1)], min_val=0, max_val=DEPTH * ROUNDS)

        early_ps = [acc[1], misc]
        arg_ps = [b_s, b_t, num[:, 1, :], num[:, 2, :]]

        block = ctx.enter_context(nc.Block())

        N_CONST = 12
        NORM_CONST = 2

        @block.sync
        def _(sp):
            for i in range(H_PARTS):
                ks = slice(i * KT // H_PARTS, (i + 1) * KT // H_PARTS)
                sp.dma_start(h_t[:, ks, :], h_in[:, ks, :]).then_inc(h_loaded[i], 16)
            sp.dma_start(prm_all[:, :, :], params).then_inc(prm_loaded, 16)
            sp.dma_start(fin_gain[:, :], norm_final).then_inc(prm_loaded, 16)

            def load_dense(l, n, slot):
                sp.wait_ge(lo_done, l * DENSE + n + 1)
                sp.dma_start(raw[:, slot, :], dense_w[l, n]).then_inc(raw_landed[slot], 16)

            def load_gu(l, q, qd, p, tiles=range(GU_TILES)):
                for i in tiles:
                    sp.wait_ge(gu_done, (qd * 2 + p) * KP + i // 2 + 1)
                    sp.dma_start(gu_slot(p, i), moe_w[l, (q * 2 + p) * PER_PAIR + i]).then_inc(gu_landed[p][i], 16)

            def load_down(l, q, qd, p):
                for i in range(2 * FT):
                    sp.wait_ge(down_split, (qd * 2 + p) * DOWN + i + 1)
                    sp.dma_start(down_slot(p, i), moe_w[l, (q * 2 + p) * PER_PAIR + GU_TILES + i])\
                      .then_inc(down_landed[p][i], 16)

            def load_quad(l, q, qd):
                load_gu(l, q, qd, 0, range(GU_TILES // 2))
                load_down(l, q, qd, 0)
                load_gu(l, q, qd, 0, range(GU_TILES // 2, GU_TILES))
                load_gu(l, q, qd, 1)
                load_down(l, q, qd, 1)

            with sp.Fori(0, DEPTH) as l:
                first = rounds_before(sp, l)
                for n in range(RING):
                    if n == 0:
                        sp.wait_ge(down_done, 2 * FT + first * QUADS * 2 * FT)
                    load_dense(l, n, n)
                with sp.Fori(0, HEADS) as h:
                    for i in range(PER_HEAD):
                        load_dense(l, RING + h * PER_HEAD + i, i % RING)
                    with sp.If(h == 0):
                        load_gu(l, 0, first * QUADS, 0)
                    with sp.If(h == 1):
                        load_gu(l, 0, first * QUADS, 1)
                    with sp.If(h == 2):
                        load_down(l, 0, first * QUADS, 0)
                load_dense(l, DENSE - 1, (DENSE - 1) % RING)
                sp.wait_ge(lo_done, RING + (l + 1) * DENSE)
                load_down(l, 0, first * QUADS, 1)
                with sp.Fori(1, QUADS) as q:
                    load_quad(l, q, first * QUADS + q)
                last = rounds_before(sp, l + 1)
                with sp.If(last > first + 1):
                    with sp.Fori(first + 1, last) as rd:
                        with sp.Fori(0, QUADS) as q:
                            load_quad(l, q, rd * QUADS + q)
            for k in range(KT):
                sp.wait_ge(x_ready, DEPTH * KT + k + 1)
                sp.dma_start(out[:, k, :], norm_buf[:, k, N_META:]).then_inc(out_stored, 16)
            sp.wait_ge(out_stored, 16 * KT)

        @block.gpsimd
        def _(pool):
            pool.memset(mean[:, :], 1.0 / D).then_inc(consts, 1)
            pool.memset(eps[:, :], EPS).then_inc(consts, 1)
            pool.memset(ones[:, :], 1.0).then_inc(consts, 1)
            pool.memset(ident[:, :], 0.0).then_inc(zeroed, 1)
            pool.memset(ahead[:, :], 0.0).then_inc(zeroed, 1)
            pool.wait_ge(zeroed, 2)
            pool.affine_select(out=ident[:, :], in_=ident[:, :], compare_op=ALU.not_equal, fill=1.0,
                               base=0, pattern=[[-1, P]], channel_multiplier=1).then_inc(consts, 1)
            pool.wait_ge(consts, NORM_CONST + 2)
            pool.tensor_copy(ident_b[:, :], ident[:, :]).then_inc(consts, 1)
            for at, w in zip(CAUSAL_AT, CAUSAL_W):
                pool.affine_select(out=ahead[:, at:at + w], in_=ahead[:, at:at + w], compare_op=ALU.is_ge,
                                   fill=FAR, base=0, pattern=[[1, w]], channel_multiplier=-1).then_inc(consts, 1)
            pool.memset(half[:, :], -0.5).then_inc(consts, 1)
            pool.tensor_copy(ident_h[:, :], ident[:, :]).then_inc(consts, 1)
            pool.memset(one_h[:, :], 1.0).then_inc(zeroed, 1)
            pool.memset(fresh[:, :], 1.0).then_inc(zeroed, 1)
            pool.wait_ge(zeroed, 4)
            pool.affine_select(out=before[:, :], in_=one_h[:, :], compare_op=ALU.is_ge, fill=0.0,
                               base=-1, pattern=[[1, P]], channel_multiplier=-1).then_inc(consts, 1)
            pool.affine_select(out=fresh[:, TT - 1:TT], in_=fresh[:, TT - 1:TT], compare_op=ALU.is_ge, fill=0.0,
                               base=-(P - T_SIZE[TT - 1]), pattern=[[0, 1]], channel_multiplier=1)\
                .then_inc(consts, 1)

            with pool.Fori(0, DEPTH) as l:
                with pool.Fori(0, HEADS) as h:
                    hd = l * HEADS + h
                    pool.wait_ge(var_ready, hd + 1)
                    pool.tensor_tensor(stat[:, 4, :], stat[:, 3, :], half[:, :], ALU.pow).then_inc(pow_ready, 1)
                pool.wait_ge(ms_tok_summed, l + 1)
                pool.tensor_tensor(rstd_tok[:, :], ms_tok[:, 0, :], half[:, :], ALU.pow).then_inc(rstd_tok_ready, 1)
        @block.scalar
        def _(act):
            def hi_dense(l, n, slot, use):
                act.wait_ge(raw_landed[slot], (ring_use(l, use, slot) + 1) * 16)
                act.wait_ge(tiles_done, l * DENSE + n + 1)
                act.activation(w_hi[:, slot, :], raw[:, slot, :], ACT.Copy, scale=W_SCALE).then_inc(hi_done, 1)

            def squares(i, ready, base):
                act.preload_act_table_set("natural_log_exp_and_others")
                for k in range(KT):
                    act.wait_ge(h_loaded[k * H_PARTS // KT], 16)
                    act.wait_ge(ready, base + k + 1)
                    act.activation(norm_buf[:, k, :], h_t[:, k, :], ACT.Square).then_inc(sq_ready, 1)

            def rms(i):
                act.wait_ge(ms_ready, i + 1)
                act.activation(rstd[:, :], misc[:, 0:T], ACT.Ln, bias=eps[:, 0:1]).then_inc(ln_ready, 1)
                act.wait_ge(ln_ready, i + 1)
                act.activation(rstd[:, :], rstd[:, :], ACT.Exp, scale=-0.5).then_inc(rstd_ready, 1)

            def norm_hi(l):
                for k in range(KT):
                    act.wait_ge(x_ready, l * KT + k + 1)
                    act.activation(x_hi[:, k, :], norm_buf[:, k, :], ACT.Copy).then_inc(x_hi_ready, 1)
                    if k == KT // 2 - 1:
                        hi_dense(l, 1, 1, 0)
                hi_dense(l, 2, 2, 0)

            def decays(l):
                act.wait_ge(a_col_ready, l + 1)
                for h in range(HEADS):
                    act.wait_ge(arg_ready, l * HEADS + h + 1)
                    for s in range(TT):
                        at, w = CAUSAL_AT[s], CAUSAL_W[s]
                        act.activation(decay[:, h, at:at + w], arg_ps[h][:, at:at + w], ACT.Exp,
                                       bias=a_col[:, s, h:h + 1], scale=-1.0).then_inc(decay_ready, 1)

            def head(l, h, first=False):
                hd = l * HEADS + h
                tile0 = l * DENSE + h * PER_HEAD
                for i in range(PER_HEAD):
                    nxt = i + 3
                    hi_dense(l, h * PER_HEAD + nxt, nxt % RING, h * 2 + nxt // RING)
                    if i == V0 + 1 and first:
                        decays(l)
                        act.preload_act_table(ACT.Sigmoid)
                    if i == V0 + 3:
                        act.wait_ge(v_turned, hd + 1)
                        act.activation(v_n[:, :, 0:DV], num[:, :, 0:DV], ACT.Copy).then_inc(v_n_ready, 1)
                    if i == CC0:
                        act.wait_ge(num_ready, hd + 1)
                        for t in range(TT):
                            act.activation(hm[:, t, :], num[:, t, 0:DV], ACT.Square,
                                           accum_out=ssq[:, t:t + 1]).then_inc(ssq_ready, 1)
                        act.activation(den[:, :], num[:, :, DV], ACT.Copy).then_inc(ssq_ready, 1)
                    if i == CB0:
                        act.wait_ge(f_ready, hd + 1)
                        for t in range(TT):
                            act.activation(hm[:, t, :], num[:, t, 0:DV], ACT.Copy,
                                           scale=stat[:, 5, t:t + 1]).then_inc(hm_ready, 1)
                    if i in (GM0, GM0 + 1, CX0, CX0 + 1, GC0, GC0 + 1):
                        act.wait_ge(tiles_done, RING + tile0 + i + 1)
                        if i == GM0:
                            act.wait_ge(ym_ready, OPEN + hd * 2)
                        if i == GC0:
                            act.wait_ge(y_ready, OPEN + hd)
                        dst, func, ready = {GM0: (sig_m, ACT.Sigmoid, sig_m_ready), CX0: (cx, ACT.Copy, cx_ready),
                                            GC0: (sig_c, ACT.Sigmoid, sig_c_ready)}[i - i % 2]
                        act.activation(dst[:, i % 2, :], acc[i % 2][:, 0:T], func, scale=UNSCALE)\
                           .then_inc(ready, 1)

            def split_down(qd, p, i):
                act.wait_ge(down_landed[p][i], (qd + 1) * 16)
                act.wait_ge(down_done, (qd * 2 + p) * FT + i // 2 + 1)
                act.activation(down_hi[p][:, i, :], down_slot(p, i), ACT.Copy, scale=W_SCALE)\
                   .then_inc(down_hi_ready, 1)

            def take_gathered(qd, side, banks=None):
                for kp in (2 * side, 2 * side + 1):
                    act.wait_ge(gathered, qd * KP + kp + 1)
                    bank = (banks or [b_s, b_t])[kp % 2]
                    for j in range(2):
                        k = 2 * kp + j
                        ins = act.activation(xg[:, k, :], bank[:, j * 4 * SLOTS:(j + 1) * 4 * SLOTS], ACT.Copy,
                                             scale=prm[:, C_FFN + k:C_FFN + k + 1])
                    ins.then_inc(xg_ready, 1)

            act.wait_ge(consts, NORM_CONST)
            act.wait_ge(padded, 1)
            with act.Fori(0, DEPTH) as l:
                first = rounds_before(act, l)
                squares(l, h_added, first * QUADS * KT)
                hi_dense(l, 0, 0, 0)
                rms(l)
                norm_hi(l)
                act.wait_ge(f_abs_ready, l + 1)
                act.activation(f_exp, f_abs, ACT.Exp, scale=-1.0)\
                   .then_inc(f_exp_ready, 1)
                act.wait_ge(f_exp_ready, l + 1)
                act.activation(f_log, f_exp, ACT.Ln, bias=1.0)\
                   .then_inc(f_log_ready, 1)
                act.wait_ge(m_row_ready, l + 1)
                act.activation(a_floor[F_ROW:GROWS, 0:T], m_row, ACT.Exp, scale=-1.0)\
                   .then_inc(floor_ready, 1)
                head(l, 0, first=True)
                with act.Fori(1, HEADS) as h:
                    head(l, h)
                for m in range(KT):
                    if m + 3 < KT:
                        n = HEADS * PER_HEAD + m + 3
                        hi_dense(l, n, n % RING, n // RING)

                for side in range(2):
                    for t in range(TT):
                        i = side * TT + t
                        act.wait_ge(h_turned, l * 2 * TT + i + 1)
                        act.activation(squared[:, i, :], wide[side][t], ACT.Square, scale=D ** -0.5,
                                       accum_out=ms_tok[:, side, t:t + 1]).then_inc(ms_tok_ready, 1)
                act.wait_ge(rstd_tok_ready, l + 1)
                for side in range(2):
                    for t in range(TT):
                        act.activation(xn_hi[:, t, side * 512:(side + 1) * 512], wide[side][t], ACT.Copy,
                                       scale=rstd_tok[:, t:t + 1]).then_inc(xn_hi_ready, 1)
                act.wait_ge(exp_in_ready, l + 1)
                act.activation(small[:, 8:13, :], small[:, 0:5, :], ACT.Exp).then_inc(exp_ready, 1)
                act.preload_act_table(ACT.Sigmoid)

                take_gathered(first * QUADS, 0, early_ps)
                take_gathered(first * QUADS, 1)
                last = rounds_before(act, l + 1)
                with act.Fori(first, last) as rd, act.Fori(0, QUADS) as q:
                    qd = rd * QUADS + q
                    for p in range(2):
                        pr = qd * 2 + p
                        if p == 0:
                            for i in range(DOWN):
                                split_down(qd, 0, i)
                        act.wait_ge(gu_done, 2 * KP + (pr + 1) * KP)
                        act.activation(sg[:, p, :], acc[p][:, 0:D_EXPERT], ACT.Sigmoid).then_inc(sg_ready, 1)
                        act.wait_ge(hid_turned, pr + 1)
                        act.activation(hid_hi[:, p, :, :],
                                       num[:, 2, p * FT * P:(p + 1) * FT * P].rearrange("p (f s) -> p f s", f=FT),
                                       ACT.Copy).then_inc(hid_hi_ready, 1)
                        for i in range(p * FT, (p + 1) * FT):
                            split_down(qd, 1, i)
                    for p in range(2):
                        pr = qd * 2 + p
                        if p == 0:
                            with act.If(qd + 1 < last * QUADS):
                                take_gathered(qd + 1, 0)
                            act.wait_ge(combined, OPEN + qd * KT)
                        act.wait_ge(down_done, 2 * FT + (pr + 1) * FT)
                        for dh in range(2):
                            act.activation(ys_hi[:, p, dh * 512:(dh + 1) * 512], y_ps(p, dh), ACT.Copy,
                                           scale=UNSCALE)\
                               .then_inc(ys_hi_ready, 1)
                    with act.If(qd + 1 < last * QUADS):
                        take_gathered(qd + 1, 1)
            squares(DEPTH, h_added, rounds_before(act, DEPTH) * QUADS * KT)
            rms(DEPTH)

        PREP, GATE, HEAD, ROUTE = 6, 6, 14, 32

        @block.vector
        def _(dve):
            dve.memset(rounds_at[:, :], 0).then_inc(rounds_ready, OPEN)
            starts = ((h_added, KT), (lo_done, RING), (tiles_done, RING), (gu_done, 2 * KP), (down_done, 2 * FT),
                      (down_split, 2 * DOWN), (sig_c_ready, 2), (ym_ready, OPEN), (hm_ready, OPEN),
                      (y_ready, OPEN), (combined, OPEN), (back_ready, OPEN), (ys_lo_ready, OPEN))
            for n, (s, count) in enumerate(starts):
                dve.memset(opened[0:1, n:n + 1], 0.0).then_inc(s, count)
            init = Chain(dve, padded, 0, 11)
            init.step(dve.memset(v_t[:, :, :], 0.0))
            init.step(dve.memset(k_t[:, :], 0.0))
            init.step(dve.memset(s_w[:, :, :], 0.0))
            init.step(dve.memset(v_n[:, :, DV:DV + 1], 1.0))
            init.step(dve.memset(u[:, :, 0:CONV_K - 1], 0.0))
            init.step(dve.memset(a_floor[:, :], 1.0))
            init.step(dve.memset(gate_hi[:, :, :], 0.0))
            init.step(dve.memset(gate_lo[:, :, :], 0.0))
            init.step(dve.memset(place[:, :], 1.0))
            init.settle()
            init.step(dve.tensor_tensor_scan(place[:, :], place[:, :], place[:, :], 0.0, ALU.mult, ALU.add))
            init.settle()
            init.step(dve.tensor_scalar(down_count[:, :], place[:, 0:EXPERTS], -33.0, None, ALU.add))
            init.end()
            for b in range(ROUNDS):
                dve.memset(limits[:, b:b + 1], float(b * SLOTS) if b else -1.0).then_inc(padded, 1)
            dve.memset(rounds_f[:, :], 0.0).then_inc(padded, 1)
            dve.wait_ge(padded, 11 + ROUNDS + 1)
            dve.wait_ge(prm_loaded, 32)
            dve.wait_ge(consts, N_CONST)

            def lo_dense(l, n, slot):
                dve.wait_ge(hi_done, l * DENSE + n + 1)
                dve.scalar_tensor_tensor(w_lo[:, slot, :], raw[:, slot, :], W_SCALE, w_hi[:, slot, :],
                                         ALU.mult, ALU.subtract).then_inc(lo_done, 1)

            def norm(i, gain, l=None):
                dve.wait_ge(rstd_ready, i + 1)

                def low(k):
                    dve.wait_ge(x_hi_ready, l * KT + k + 1)
                    dve.tensor_tensor(x_lo[:, k, :], norm_buf[:, k, :], x_hi[:, k, :], ALU.subtract)\
                       .then_inc(x_lo_ready, 1)
                for k in range(KT):
                    dve.scalar_tensor_tensor(norm_buf[:, k, :], h_t[:, k, :], gain[:, k:k + 1], rstd[:, :],
                                             ALU.mult, ALU.mult).then_inc(x_ready, 1)
                    if l is not None and k:
                        low(k - 1)
                    if l is not None and k == KT // 2:
                        lo_dense(l, 0, 0)
                if l is not None:
                    low(KT - 1)

            def pick_g(l):
                g = Chain(dve, pick_step, l * TT, TT)
                for s in range(TT):
                    at, w = CAUSAL_AT[s], CAUSAL_W[s]
                    g.step(dve.tensor_copy(g_pick[:, 0, at:at + w], g_max[:, T_START[s]:T]))
                g.settle()
                for h in reversed(range(HEADS)):
                    dve.tensor_scalar(g_pick[:, h, :], g_pick[:, 0, :], ident[0:HEADS, h:h + 1], None, ALU.mult)\
                       .then_inc(pick_ready, 1)
                g.end()

            def split_down(qd, p, i):
                number = qd * 2 * DOWN + p * DOWN + i
                dve.wait_ge(down_hi_ready, number + 1)
                dve.scalar_tensor_tensor(down_lo[p][:, i, :], down_slot(p, i), W_SCALE, down_hi[p][:, i, :],
                                         ALU.mult, ALU.subtract).then_inc(down_split, 1)

            def fill_slots(l, qd, q):
                four = bass.ds(q * 4, 4)
                dve.wait_ge(pos_ready, qd + l + 1)
                dve.tensor_tensor(pick[:, :, :].rearrange("p t (e s) -> p t e s", e=4),
                                  place[:, :].unsqueeze(1).unsqueeze(1).broadcast_to([P, TT, 4, SLOTS]),
                                  pos1[:, :, four].unsqueeze(3).broadcast_to([P, TT, 4, SLOTS]), ALU.is_equal)\
                   .then_inc(picked, 1)
                dve.wait_ge(picked, qd + 1)
                dve.tensor_tensor(pick[LOW_ROWS, TT - 1, :].rearrange("p (e s) -> p e s", e=4),
                                  place[NEW_ROWS, :].unsqueeze(1).broadcast_to([32, 4, SLOTS]),
                                  pos1[NEW_ROWS, TT - 1, four].unsqueeze(2).broadcast_to([32, 4, SLOTS]), ALU.is_equal)\
                   .then_inc(pick_ready_q, 1)
                dve.wait_ge(pick_ready_q, qd + 1)
                dve.tensor_scalar(pos1[:, :, four], pos1[:, :, four], float(-SLOTS), None, ALU.add)\
                   .then_inc(pos_ready, 1)

            def fill_gates(qd, q):
                four = bass.ds(q * 4, 4)
                dve.tensor_scalar(gate_q[:, 0, :, :], gate_n[:, :, four], 1.0, None, ALU.mult)\
                   .then_inc(gate_q_ready, 1)
                dve.wait_ge(gate_q_ready, qd * 2 + 1)
                dve.tensor_tensor(gate_q[:, 1, :, :], gate_n[:, :, four], gate_q[:, 0, :, :], ALU.subtract)\
                   .then_inc(gate_q_ready, 1)

            dve.wait_ge(rounds_ready, OPEN)
            with dve.Fori(0, DEPTH) as l:
                prep = Chain(dve, prep_done, l * PREP, PREP)
                prep.step(dve.tensor_scalar(prm[:, :], prm_all[:, l, :], 1.0, None, ALU.mult))
                prep.settle()
                gw = prm[:, C_GATE:C_ROUTE].rearrange("p (k g) -> p k g", k=KT)
                for g, row in ((0, 0), (HEADS, F_ROW)):
                    prep.step(dve.tensor_scalar(gate_hi[:, :, row:row + HEADS], gw[:, :, g:g + HEADS], W_SCALE, None,
                                                ALU.mult))
                prep.settle()
                for g, row in ((0, 0), (HEADS, F_ROW)):
                    prep.step(dve.scalar_tensor_tensor(gate_lo[:, :, row:row + HEADS], gw[:, :, g:g + HEADS], W_SCALE,
                                                       gate_hi[:, :, row:row + HEADS], ALU.mult, ALU.subtract))
                prep.step(dve.tensor_tensor(route_w[:, :, :],
                                            prm[:, C_ROUTE:C_BIF].rearrange("p (k n) -> p k n", k=KT),
                                            prm[:, C_FFN:C_FFN + KT].unsqueeze(2).broadcast_to([P, KT, N_ROUTE]),
                                            ALU.mult))
                prep.end()
                norm(l, prm[:, C_MIX:C_MIX + KT], l)
                lo_dense(l, 1, 1)

                dve.wait_ge(gates_ready, l + 1)
                g = Chain(dve, gate_step, l * GATE, GATE)
                g.step(dve.tensor_scalar(i_gate, misc[0:HEADS, 0:T], UNSCALE, prm[0:HEADS, C_BIF:C_BIF + 1],
                                         ALU.mult, ALU.add))
                g.step(dve.tensor_scalar(f_gate, misc[F_ROW:GROWS, 0:T], UNSCALE,
                                         prm[F_ROW:GROWS, C_BIF:C_BIF + 1], ALU.mult, ALU.add))
                g.settle()
                dve.scalar_tensor_tensor(f_abs, f_gate, -1.0, f_gate, ALU.mult, ALU.max)\
                   .then_inc(f_abs_ready, 1)
                dve.wait_ge(f_log_ready, l + 1)
                g.step(dve.scalar_tensor_tensor(f_log, f_gate, 0.0,
                                                f_log, ALU.min, ALU.subtract))
                g.settle()
                g.step(dve.tensor_tensor_scan(f_sum, ones[F_ROW:GROWS, 0:1].broadcast_to([HEADS, T]), f_log, 0.0,
                                              ALU.mult, ALU.add))
                g.settle()
                g.step(dve.tensor_tensor(a_floor[0:HEADS, 0:T], i_gate, f_sum, ALU.subtract))
                g.settle()
                g.step(dve.tensor_tensor_scan(g_max, a_floor[0:HEADS, 0:T], a_floor[0:HEADS, 0:T], 0.0,
                                              ALU.max, ALU.max))
                g.settle()
                dve.tensor_tensor(m_row, f_sum, g_max, ALU.add).then_inc(m_row_ready, 1)
                g.end()

                with dve.Fori(0, HEADS) as h:
                    hd = l * HEADS + h
                    tile0 = l * DENSE + h * PER_HEAD
                    c = Chain(dve, head_step, hd * HEAD, HEAD)
                    for i in range(PER_HEAD):
                        nxt = i + 2
                        if i != CB0:
                            lo_dense(l, h * PER_HEAD + nxt, nxt % RING)
                        b, ct = acc[i % 2][:, 0:T], i % 2
                        if i in (Q, K, V0, V0 + 1, CC0, CC0 + 1, CB0, CB0 + 1):
                            dve.wait_ge(tiles_done, RING + tile0 + i + 1)
                        if i in (Q, K, V0, V0 + 1):
                            dst = {Q: q_t[:, :], K: k_t[:, 0:T], V0: v_t[:, 0, 0:T], V0 + 1: v_t[:, 1, 0:T]}[i]
                            dve.tensor_scalar(dst, b, UNSCALE, None, ALU.mult).then_inc(qkv_ready, 1)
                        if i == Q:
                            with dve.If(h == 0):
                                pick_g(l)
                        if i == V0:
                            with dve.If(h == 0):
                                dve.wait_ge(a_col_ps, l + 1)
                                dve.tensor_copy(a_col[:, :, :],
                                                misc[:, 0:TP].rearrange("p (t g) -> p t g", t=TT)[:, :, 0:GROWS])\
                                   .then_inc(a_col_ready, 1)
                        if i == GM0 + 1:
                            dve.wait_ge(scores_ready, hd + 1)
                            dve.wait_ge(decay_ready, (l + 1) * HEADS * TT)
                            for s in range(TT):
                                at, w = CAUSAL_AT[s], CAUSAL_W[s]
                                dve.scalar_tensor_tensor(s_w[:, s, T_START[s]:T], b_s[:, at:at + w], P ** -0.5,
                                                         decay[:, h, at:at + w], ALU.mult, ALU.mult)\
                                   .then_inc(s_w_ready, 1)
                        if i in (CC0, CC0 + 1):
                            dve.wait_ge(cx_ready, hd * 2 + ct + 1)
                            dve.scalar_tensor_tensor(u[:, ct, CONV_K - 1:], b, UNSCALE, cx[:, ct, :],
                                                     ALU.mult, ALU.mult).then_inc(cc_read, 1)
                            dve.wait_ge(cc_read, hd * 2 + ct + 1)
                            tap = [prm[:, C_CONV + j * KT:C_CONV + (j + 1) * KT] for j in range(CONV_K)]
                            c.step(dve.tensor_scalar(cv[:, ct, :], u[:, ct, 0:T], tap[0][:, bass.ds(h * 2 + ct, 1)],
                                                     None, ALU.mult))
                            if ct:
                                dve.wait_ge(ssq_ready, (hd + 1) * (TT + 1))
                                c.step(dve.scalar_tensor_tensor(stat[:, 0, :], den[:, :], -1.0, den[:, :],
                                                                ALU.mult, ALU.max))
                            for j in range(1, CONV_K):
                                c.settle()
                                c.step(dve.scalar_tensor_tensor(cv[:, ct, :], u[:, ct, j:j + T],
                                                                tap[j][:, bass.ds(h * 2 + ct, 1)], cv[:, ct, :],
                                                                ALU.mult, ALU.add))
                                if ct and j == 1:
                                    dve.wait_ge(a_col_ready, l + 1)
                                    c.step(dve.tensor_tensor(stat[:, 0, :], stat[:, 0, :],
                                                             a_col[:, :, bass.ds(F_ROW + h, 1)]
                                                             .rearrange("p t o -> p (t o)"), ALU.max))
                                if ct and j == 2:
                                    c.step(dve.reciprocal(stat[:, 1, :], stat[:, 0, :]))
                            if ct:
                                c.settle()
                                c.step(dve.tensor_tensor(stat[:, 2, :], ssq[:, :], stat[:, 1, :], ALU.mult))
                                c.settle()
                                c.step(dve.tensor_tensor(stat[:, 2, :], stat[:, 2, :], stat[:, 1, :], ALU.mult))
                                c.settle()
                                dve.tensor_scalar(stat[:, 3, :], stat[:, 2, :], 1.0 / DV, EPS, ALU.mult, ALU.add)\
                                   .then_inc(var_ready, 1)
                        if i in (CB0, CB0 + 1):
                            c.settle()
                            dve.scalar_tensor_tensor(cv[:, ct, :], b, UNSCALE, cv[:, ct, :],
                                                     ALU.mult, ALU.mult).then_inc(cb_read, 1)
                        if i == CB0:
                            lo_dense(l, h * PER_HEAD + nxt, nxt % RING)
                            dve.wait_ge(pow_ready, hd + 1)
                            dve.tensor_tensor(stat[:, 5, :], stat[:, 1, :], stat[:, 4, :], ALU.mult)\
                               .then_inc(f_ready, 1)
                        if i == GC0 + 1:
                            dve.wait_ge(hm_turned, hd + 1)
                            dve.wait_ge(sig_m_ready, (hd + 1) * 2)
                            for v, bank in enumerate((b_s, b_t)):
                                dve.scalar_tensor_tensor(ym[:, v, :], bank[:, 0:T],
                                                         prm[:, bass.ds(C_GAIN + h * 2 + v, 1)],
                                                         sig_m[:, v, :], ALU.mult, ALU.mult).then_inc(ym_ready, 1)
                    dve.wait_ge(sig_c_ready, 2 + (hd + 1) * 2)
                    dve.wait_ge(cb_read, (hd + 1) * 2)
                    c.step(dve.tensor_tensor(cv[:, :, :], cv[:, :, :], sig_c[:, :, :], ALU.mult))
                    c.settle()
                    dve.wait_ge(ym_ready, OPEN + (hd + 1) * 2)
                    c.step(dve.tensor_tensor(ym[:, :, :], cv[:, :, :], ym[:, :, :], ALU.add))
                    c.settle()
                    c.step(dve.tensor_scalar(y_hi[:, bass.ds(h * 2, 2), :], ym[:, :, :], 1.0, None, ALU.mult))
                    c.settle()
                    dve.tensor_tensor(y_lo[:, bass.ds(h * 2, 2), :], ym[:, :, :], y_hi[:, bass.ds(h * 2, 2), :],
                                      ALU.subtract).then_inc(y_ready, 1)
                    c.end()

                for m in range(KT):
                    n = HEADS * PER_HEAD + m
                    if m + 2 < KT:
                        lo_dense(l, n + 2, (n + 2) % RING)
                    dve.wait_ge(tiles_done, RING + l * DENSE + n + 1)
                    dve.scalar_tensor_tensor(h_t[:, m, :], acc[n % 2][:, 0:T], UNSCALE, h_t[:, m, :],
                                             ALU.mult, ALU.add).then_inc(h_mixed, 1)

                first = rounds_before(dve, l)
                r = Chain(dve, route_step, l * ROUTE, ROUTE)

                def then(ins):
                    r.step(ins)
                    r.settle()

                dve.wait_ge(ms_tok_ready, (l + 1) * 2 * TT)
                dve.scalar_tensor_tensor(ms_tok[:, 0, :], ms_tok[:, 0, :], EPS, ms_tok[:, 1, :], ALU.add, ALU.add)\
                   .then_inc(ms_tok_summed, 1)
                dve.wait_ge(rstd_tok_ready, l + 1)

                dve.wait_ge(logits_ready, l + 1)

                def spread(column, n):
                    return column.unsqueeze(2).broadcast_to([P, TT, n])

                then(dve.tensor_tensor(lg[:, :, :], misc[:, 0:TT * N_ROUTE].rearrange("p (t g) -> p t g", t=TT),
                                       spread(rstd_tok[:, :], N_ROUTE), ALU.mult))
                then(dve.tensor_tensor(lg[:, :, :], lg[:, :, :],
                                       prm[:, C_BROUTE:C_ALL].unsqueeze(1).broadcast_to([P, TT, N_ROUTE]), ALU.add))
                sets = lg[:, :, :].rearrange("p t (s e) -> p t s e", e=PER_GROUP)
                gl, el = lg[:, :, 0:N_GROUPS], lg[:, :, N_GROUPS:]

                def col(i):
                    return small[:, i, :]

                def by_group(x):
                    return x.rearrange("p t (g e) -> p t g e", e=PER_GROUP)

                def first_max(values, n, best, at, pick, tmp):
                    shape = [P, TT, n, PER_GROUP]
                    count = down_count[:, 0:PER_GROUP].unsqueeze(1).unsqueeze(1).broadcast_to(shape)
                    then(dve.tensor_reduce(best, values, AX.X, ALU.max))
                    then(dve.tensor_tensor(tmp, values, best.unsqueeze(3).broadcast_to(shape), ALU.is_equal))
                    then(dve.tensor_tensor(tmp, tmp, count, ALU.mult))
                    then(dve.tensor_reduce(at, tmp, AX.X, ALU.min))
                    then(dve.tensor_tensor(pick, count, at.unsqueeze(3).broadcast_to(shape), ALU.is_equal))

                top, tmp, others, second_e, both, bests, more = (rt[:, i, :, :] for i in range(7))
                group, first_e = top[:, :, 0:N_GROUPS], top[:, :, N_GROUPS:]
                others, second_e, both = (x[:, :, 0:EXPERTS] for x in (others, second_e, both))
                best1, at1, best2, at2 = (bests[:, :, i:j] for i, j in ((0, 5), (5, 10), (10, 14), (14, 18)))
                group_once, gap, chosen_gap = (more[:, :, i:i + N_GROUPS] for i in (0, 4, 8))

                def over_group(x):
                    return x.unsqueeze(3).broadcast_to([P, TT, N_GROUPS, PER_GROUP])

                first_max(sets, 1 + N_GROUPS, best1, at1, by_group(top), by_group(tmp))
                r.step(dve.tensor_tensor(group_once, group, spread(fresh[:, :], N_GROUPS), ALU.mult))
                then(dve.scalar_tensor_tensor(others, first_e, -FAR, el, ALU.mult, ALU.add))
                first_max(by_group(others), N_GROUPS, best2, at2, by_group(second_e), by_group(tmp[:, :, 0:EXPERTS]))
                then(dve.tensor_tensor(both, first_e, second_e, ALU.add))
                dve.tensor_tensor(by_group(sel[:, :, :]), by_group(both), over_group(group_once), ALU.mult)\
                   .then_inc(sel_ready, 1)
                r.step(dve.tensor_tensor(small[:, 0:4, :].rearrange("p g t -> p t g"), gl,
                                         best1[:, :, 0:1].broadcast_to([P, TT, N_GROUPS]), ALU.subtract))
                then(dve.tensor_tensor(gap, best2, best1[:, :, 1:], ALU.subtract))
                then(dve.tensor_tensor(chosen_gap, gap, group, ALU.mult))
                dve.tensor_reduce(col(4), chosen_gap, AX.X, ALU.add).then_inc(exp_in_ready, 1)

                def xn_low(side):
                    for t in range(TT):
                        cols = slice(side * 512, (side + 1) * 512)
                        dve.wait_ge(xn_hi_ready, l * 2 * TT + side * TT + t + 1)
                        rows, dst = (slice(0, P), xn_lo[:, t, cols]) if t < TT - 1 else \
                            (NEW_ROWS, xn_hi[LOW_ROWS, t, cols])
                        dve.scalar_tensor_tensor(dst, wide[side][t][rows, :], rstd_tok[rows, t:t + 1],
                                                 xn_hi[rows, t, cols], ALU.mult, ALU.subtract).then_inc(xn_lo_ready, 1)

                dve.wait_ge(pos_ps, l + 1)
                dve.scalar_tensor_tensor(pos1[:, :, :], misc[:, 0:TT * EXPERTS].rearrange("p (t e) -> p t e", t=TT),
                                         1.0, sel[:, :, :], ALU.add, ALU.mult).then_inc(pos_ready, 1)
                r.step(dve.tensor_reduce(busiest[:, :], misc[:, TT * EXPERTS:(TT + 1) * EXPERTS], AX.X, ALU.max))
                fill_slots(l, first * QUADS, 0)
                xn_low(0)
                xn_low(1)
                r.settle()
                then(dve.tensor_tensor(needed[:, :], limits[:, :], busiest[:, :].broadcast_to([P, ROUNDS]), ALU.is_lt))
                then(dve.tensor_reduce(rounds_n[:, :], needed[:, :], AX.X, ALU.add))
                then(dve.tensor_tensor(rounds_f[:, :], rounds_f[:, :], rounds_n[:, :], ALU.add))
                dve.tensor_scalar(rounds_at[:, bass.ds(l + 1, 1)], rounds_f[:, :], 1.0, None, ALU.mult)\
                   .then_inc(rounds_ready, 1)
                dve.wait_ge(exp_ready, l + 1)
                e, groups_sum, one_e, w1, w2 = col(12), col(20), col(21), col(22), col(23)
                then(dve.tensor_reduce(groups_sum, small[:, 8:12, :].rearrange("p g t -> p t g"), AX.X, ALU.add))
                then(dve.tensor_scalar(one_e, e, 1.0, None, ALU.add))
                then(dve.tensor_tensor(groups_sum, groups_sum, one_e, ALU.mult))
                then(dve.reciprocal(w1, groups_sum))
                then(dve.tensor_tensor(w2, w1, e, ALU.mult))
                then(dve.tensor_tensor(first_e, first_e, spread(w1, EXPERTS), ALU.mult))
                then(dve.tensor_tensor(second_e, second_e, spread(w2, EXPERTS), ALU.mult))
                dve.wait_ge(rounds_ready, OPEN + l + 1)
                then(dve.tensor_tensor(both, first_e, second_e, ALU.add))
                then(dve.tensor_tensor(by_group(gate_n[:, :, :]), by_group(both), over_group(group), ALU.mult))
                then(dve.memset(gate_n[LOW_ROWS, TT - 1, :], 0.0))
                fill_gates(first * QUADS, 0)
                r.end()
                last = rounds_before(dve, l + 1)
                with dve.Fori(first, last) as rd:
                    with dve.Fori(0, QUADS) as q:
                        qd = rd * QUADS + q
                        dve.wait_ge(slots_ps, qd + 1)
                        for e in range(2):
                            rows = slice(e * SLOTS, (e + 1) * SLOTS)
                            dve.tensor_copy(slot_gate[rows, :],
                                            misc[rows, 0:4].rearrange("p (a e) -> p a e", e=2)[:, :, e])\
                               .then_inc(slot_gate_ready, 1)
                        dve.tensor_copy(back[:, :, :],
                                        misc_h[:, BACK_AT:BACK_AT + 2 * T].rearrange("p (a t) -> p a t", a=2))\
                           .then_inc(back_ready, 1)
                        dve.wait_ge(slot_gate_ready, (qd + 1) * 2)
                        for i in range(DOWN):
                            split_down(qd, 0, i)
                        for p in range(2):
                            pr = qd * 2 + p
                            dve.wait_ge(sg_ready, pr + 1)
                            dve.tensor_tensor(sg[:, p, :], acc[p][:, 0:D_EXPERT], sg[:, p, :], ALU.mult)\
                               .then_inc(silu_ready, 1)
                            dve.wait_ge(silu_ready, pr + 1)
                            dve.scalar_tensor_tensor(hid[:, p, :], acc[p][:, D_EXPERT:], slot_gate[:, p:p + 1],
                                                     sg[:, p, :], ALU.mult, ALU.mult).then_inc(hid_ready, 1)
                            dve.wait_ge(hid_hi_ready, pr + 1)
                            turned = num[:, 2, p * FT * P:(p + 1) * FT * P]
                            dve.tensor_tensor(hid_lo[:, p, :, :], turned.rearrange("p (f s) -> p f s", f=FT),
                                              hid_hi[:, p, :, :], ALU.subtract).then_inc(hid_lo_ready, 1)
                            if p == 0:
                                with dve.If(qd + 1 < last * QUADS):
                                    fill_slots(l, qd + 1, (q + 1) % QUADS)
                                    fill_gates(qd + 1, (q + 1) % QUADS)
                            for i in range(p * FT, (p + 1) * FT):
                                split_down(qd, 1, i)
                        for p in range(2):
                            for dh in range(2):
                                cols = slice(dh * 512, (dh + 1) * 512)
                                dve.wait_ge(ys_hi_ready, qd * 4 + p * 2 + dh + 1)
                                dve.scalar_tensor_tensor(ys_lo[:, p, cols], y_ps(p, dh), UNSCALE, ys_hi[:, p, cols],
                                                         ALU.mult, ALU.subtract)\
                                   .then_inc(ys_lo_ready, 1)
                        dve.wait_ge(h_added, KT + qd * KT)
                        for m in range(KT):
                            dve.wait_ge(combined, OPEN + qd * KT + m + 1)
                            dve.tensor_tensor(h_t[:, m, :], num[:, (m + 2) % 3, 0:T], h_t[:, m, :], ALU.add)\
                               .then_inc(h_added, 1)
            norm(DEPTH, fin_gain)

        @block.tensor
        def _(pe):
            pe.wait_ge(consts, NORM_CONST)

            def mean_square(i, k):
                pe.wait_ge(sq_ready, i * KT + k + 1)
                mm = pe.matmul(misc[:, 0:T], mean[:, :], norm_buf[:, k, :], start=(k == 0), stop=(k == KT - 1))
                if k == KT - 1:
                    mm.then_inc(ms_ready, 1)

            def three(dst, hi, lo, rhi, rlo, first, last):
                pe.matmul(dst, hi, rhi, start=first, stop=False)
                pe.matmul(dst, hi, rlo, start=False, stop=False)
                return pe.matmul(dst, lo, rhi, start=False, stop=last)

            def dense(l, n, slot, bank, rhi, rlo, ks=range(KT)):
                pe.wait_ge(lo_done, RING + l * DENSE + n + 1)
                for k in ks:
                    cols = slice(k * P, (k + 1) * P)
                    mm = three(acc[bank][:, 0:T], w_hi[:, slot, cols], w_lo[:, slot, cols], rhi[:, k, :], rlo[:, k, :],
                               k == 0, k == KT - 1)
                if ks.stop == KT:
                    mm.then_inc(tiles_done, 1)

            def decay_arguments(l):
                pe.wait_ge(floor_ready, l + 1)
                for t in range(TT):
                    mm = pe.transpose(misc[:, t * P:(t + 1) * P], a_floor[:, t * P:(t + 1) * P], ident[:, :])
                mm.then_inc(a_col_ps, 1)
                pe.wait_ge(pick_ready, (l + 1) * HEADS)
                for h in range(HEADS):
                    pe.matmul(arg_ps[h][:, 0:CAUSAL], ones[0:HEADS, :], g_pick[:, h, :], start=True, stop=False)
                    pe.matmul(arg_ps[h][:, 0:CAUSAL], ident_b[:, :], ahead[:, :], start=False, stop=True)\
                      .then_inc(arg_ready, 1)

            def turn_h(l, k):
                pe.wait_ge(h_mixed, l * KT + k + 1)
                for t in range(TT):
                    mm = pe.matmul(misc[:, t * N_ROUTE:(t + 1) * N_ROUTE], h_t[:, k, R_START[t]:R_START[t] + P],
                                   route_w[:, k, :], start=(k == 0 and t == 0), stop=(k == KT - 1),
                                   skip_group_check=True)
                if k == KT - 1:
                    mm.then_inc(logits_ready, 1)
                side, j = divmod(k, 4)
                for t in range(TT):
                    ks = [k] if (side, t) != (1, TT - 1) else range(4, KT) if k == KT - 1 else []
                    for kk in ks:
                        at = kk % 4 * P
                        mm = pe.transpose(wide[side][t][:, at:at + P], h_t[:, kk, R_START[t]:R_START[t] + P],
                                          ident[:, :])
                        if kk % 4 == 3:
                            mm.then_inc(h_turned, 1)

            def combine(qd, norm=None):
                def pair(m, p):
                    for part in (ys_hi, ys_lo):
                        mm = pe.matmul(num[:, (m + 2) % 3, 0:T], part[:, p, m * P:(m + 1) * P], back[:, p, :],
                                       start=(p == 0 and part is ys_hi), stop=(p == 1 and part is ys_lo))
                    return mm
                pe.wait_ge(back_ready, OPEN + qd + 1)
                pe.wait_ge(ys_lo_ready, OPEN + qd * 4 + 2)
                for m in range(TT):
                    pair(m, 0)
                pe.wait_ge(ys_lo_ready, OPEN + (qd + 1) * 4)
                for m in range(KT):
                    if m >= TT:
                        pe.wait_ge(h_added, KT + qd * KT + m - 2)
                        pair(m, 0)
                    pair(m, 1).then_inc(combined, 1)
                    if norm is not None and m >= 2:
                        mean_square(norm, m - 2)
                if norm is not None:
                    mean_square(norm, KT - 2)
                    mean_square(norm, KT - 1)

            HIGH = [(xn_hi, t) for t in range(TT - 1)]
            LOW = [(xn_lo, t) for t in range(TT - 1)] + [(xn_hi, TT - 1)]

            def gather(qd, side):
                if side == 0:
                    pe.wait_ge(pick_ready_q, qd + 1)
                for k in range(side * KT // 2, (side + 1) * KT // 2):
                    bank = [b_s, b_t][k // 2 % 2]
                    if k % 2 == 0 and k >= 4:
                        pe.wait_ge(xg_ready, qd * KP + k // 2 - 1)
                    for i, (part, t) in enumerate(HIGH + LOW):
                        mm = pe.matmul(bank[:, k % 2 * 4 * SLOTS:(k % 2 + 1) * 4 * SLOTS],
                                       part[:, t, k * P:(k + 1) * P], pick[:, t, :], start=(i == 0),
                                       stop=(i == len(HIGH + LOW) - 1), skip_group_check=True)
                    if k % 2:
                        mm.then_inc(gathered, 1)

            def turn_slots(qd):
                pe.wait_ge(gate_q_ready, (qd + 1) * 2)
                pe.wait_ge(back_ready, OPEN + qd)
                for p in range(2):
                    cols = slice(p * 2 * SLOTS, (p + 1) * 2 * SLOTS)
                    for t in range(TT):
                        for part in range(2):
                            pe.matmul(misc[:, 2 * p:2 * p + 2], pick[:, t, cols], gate_q[:, part, t, 2 * p:2 * p + 2],
                                      start=(t == 0 and part == 0), stop=(t == TT - 1 and part == 1),
                                      skip_group_check=True)
                for p in range(2):
                    cols = slice(p * 2 * SLOTS, (p + 1) * 2 * SLOTS)
                    for t in reversed(range(TT)):
                        at = BACK_AT + p * T + R_START[t]
                        mm = pe.transpose(misc_h[:, at:at + P], pick[:, t, cols], ident_h[:, :])
                mm.then_inc(slots_ps, 1)

            def turn_hid(qd, p):
                pe.wait_ge(hid_ready, qd * 2 + p + 1)
                for f in range(FT):
                    mm = pe.transpose(num[:, 2, (p * FT + f) * P:(p * FT + f + 1) * P], hid[:, p, f * P:(f + 1) * P],
                                      ident[:, :])
                mm.then_inc(hid_turned, 1)

            def down(qd, p):
                pe.wait_ge(hid_lo_ready, qd * 2 + p + 1)
                for f in range(FT):
                    pe.wait_ge(down_split, 2 * DOWN + qd * 2 * DOWN + p * DOWN + (f + 1) * 2)
                    for dh in range(2):
                        for part, (w, hid_part) in enumerate(((down_hi, hid_hi), (down_hi, hid_lo), (down_lo, hid_hi))):
                            for e in range(2):
                                rows = slice(e * SLOTS, (e + 1) * SLOTS)
                                mm = pe.matmul(y_ps(p, dh)[rows, :], hid_part[:, p, f, rows],
                                               w[p][:, f * 2 + e, dh * 512:(dh + 1) * 512],
                                               start=(f == 0 and part == 0), stop=(f == FT - 1 and part == 2),
                                               skip_group_check=True)
                    mm.then_inc(down_done, 1)

            for k in range(KT):
                mean_square(0, k)
            pe.wait_ge(consts, N_CONST)
            pe.wait_ge(padded, 11 + ROUNDS + 1)
            with pe.Fori(0, DEPTH) as l:
                pe.wait_ge(prep_done, (l + 1) * PREP)
                pe.wait_ge(rstd_ready, l + 1)
                for k in range(KT):
                    pe.wait_ge(x_lo_ready, l * KT + k + 1)
                    mm = three(misc[0:GROWS, 0:T], gate_hi[:, k, :], gate_lo[:, k, :], x_hi[:, k, :], x_lo[:, k, :],
                               k == 0, k == KT - 1)
                mm.then_inc(gates_ready, 1)
                with pe.Fori(0, HEADS) as h:
                    hd = l * HEADS + h
                    for i in range(PER_HEAD):
                        prev = (i - 2) % PER_HEAD
                        if i < 2:
                            pe.wait_ge(sig_c_ready, 1 + i + hd * 2)
                        elif prev < GM0:
                            pe.wait_ge(qkv_ready, hd * 4 + prev + 1)
                        else:
                            read = {GM0: sig_m_ready, CX0: cx_ready, CC0: cc_read, CB0: cb_read}[prev - prev % 2]
                            pe.wait_ge(read, hd * 2 + prev % 2 + 1)
                        dense(l, h * PER_HEAD + i, i % RING, i % 2, x_hi, x_lo)
                        if i == V0:
                            with pe.If(h == 0):
                                decay_arguments(l)
                        if i == GM0:
                            pe.wait_ge(qkv_ready, hd * 4 + 4)
                            pe.wait_ge(decay_ready, (l + 1) * HEADS * TT)
                            pe.wait_ge(hm_ready, OPEN + hd * TT)
                            for t in range(TT):
                                for v in range(2):
                                    mm = pe.transpose(num[:, t, v * P:(v + 1) * P], v_t[:, v, t * P:(t + 1) * P],
                                                      ident[:, :])
                            mm.then_inc(v_turned, 1)
                            pe.wait_ge(ym_ready, OPEN + hd * 2)
                            pe.wait_ge(decay_ready, (l + 1) * HEADS * TT)
                            for s in range(TT):
                                mm = pe.matmul(b_s[:, CAUSAL_AT[s]:CAUSAL_AT[s] + CAUSAL_W[s]],
                                               k_t[:, s * P:(s + 1) * P], q_t[:, T_START[s]:T],
                                               start=(s == 0), stop=(s == TT - 1), skip_group_check=True)
                            mm.then_inc(scores_ready, 1)
                        if i == CX0 + 1:
                            pe.wait_ge(s_w_ready, (hd + 1) * TT)
                            pe.wait_ge(v_n_ready, hd + 1)
                            for t in range(TT):
                                for s in range(t + 1):
                                    mm = pe.matmul(num[:, t, 0:DV + 1], s_w[0:T_SIZE[s], s, t * P:(t + 1) * P],
                                                   v_n[0:T_SIZE[s], s, :], start=(s == 0), stop=(s == t))
                            mm.then_inc(num_ready, 1)
                        if i == GC0:
                            pe.wait_ge(hm_ready, OPEN + (hd + 1) * TT)
                            for v, bank in enumerate((b_s, b_t)):
                                for t in range(TT):
                                    mm = pe.transpose(bank[:, t * P:t * P + T_SIZE[t]],
                                                      hm[0:T_SIZE[t], t, v * P:(v + 1) * P],
                                                      ident[0:T_SIZE[t], 0:T_SIZE[t]])
                            mm.then_inc(hm_turned, 1)

                early = (HEADS - 1) * DV // P
                pe.wait_ge(y_ready, OPEN + (l + 1) * HEADS - 1)
                pe.wait_ge(sig_c_ready, 2 + (l + 1) * HEADS * 2)
                for ks in (range(early), range(early, KT)):
                    for m in range(2):
                        if m == 0 and ks.start:
                            pe.wait_ge(y_ready, OPEN + (l + 1) * HEADS)
                        dense(l, HEADS * PER_HEAD + m, m, m, y_hi, y_lo, ks)
                for m in range(2, KT):
                    n = HEADS * PER_HEAD + m
                    pe.wait_ge(h_mixed, l * KT + m - 1)
                    dense(l, n, n % RING, n % 2, y_hi, y_lo)
                    turn_h(l, m - 2)
                turn_h(l, KT - 2)
                turn_h(l, KT - 1)

                pe.wait_ge(sel_ready, l + 1)
                for t in range(TT):
                    for s in range(t + 1):
                        mm = pe.matmul(misc[:, t * EXPERTS:(t + 1) * EXPERTS], (before if s == t else one_h)[:, :],
                                       sel[:, s, :], start=(s == 0), stop=(s == t))
                for s in range(TT):
                    mm = pe.matmul(misc[:, TT * EXPERTS:(TT + 1) * EXPERTS], one_h[:, :], sel[:, s, :],
                                   start=(s == 0), stop=(s == TT - 1))
                mm.then_inc(pos_ps, 1)

                first = rounds_before(pe, l)
                pe.wait_ge(picked, first * QUADS + 1)
                pe.wait_ge(xn_hi_ready, l * 2 * TT + TT)
                for parts in (HIGH, LOW):
                    if parts is LOW:
                        pe.wait_ge(pick_ready_q, first * QUADS + 1)
                        pe.wait_ge(xn_lo_ready, l * 2 * TT + TT)
                    for k in range(KT // 2):
                        for part, t in parts:
                            mm = pe.matmul(early_ps[k // 2][:, k % 2 * 4 * SLOTS:(k % 2 + 1) * 4 * SLOTS],
                                           part[:, t, k * P:(k + 1) * P], pick[:, t, :],
                                           start=(k % 2 == 0 and t == 0 and part is xn_hi),
                                           stop=(t == TT - 1), skip_group_check=True)
                        if k % 2 and parts is LOW:
                            mm.then_inc(gathered, 1)
                pe.wait_ge(xn_lo_ready, (l + 1) * 2 * TT)
                gather(first * QUADS, 1)
                pe.wait_ge(xg_ready, first * QUADS * KP + KP // 2)
                last = rounds_before(pe, l + 1)
                turn_slots(first * QUADS)
                with pe.Fori(first, last) as rd, pe.Fori(0, QUADS) as q:
                    qd = rd * QUADS + q
                    pe.wait_ge(ys_lo_ready, OPEN + qd * 4)
                    for p in range(2):
                        for kp in range(KP):
                            if p == 1 and kp == 2:
                                pe.wait_ge(h_added, KT + qd * KT)
                                turn_hid(qd, 0)
                            if p == 0:
                                pe.wait_ge(xg_ready, qd * KP + kp + 1)
                            for e in range(2):
                                pe.wait_ge(gu_landed[p][kp * 2 + e], (qd + 1) * 16)
                            for k in (2 * kp, 2 * kp + 1):
                                for e in range(2):
                                    at = (p * 2 + e) * SLOTS
                                    mm = pe.matmul(acc[p][e * SLOTS:(e + 1) * SLOTS, :], xg[:, k, at:at + SLOTS],
                                                   gu_slot(p, kp * 2 + e)[:, k % 2 * 512:(k % 2 + 1) * 512],
                                                   start=(k == 0), stop=(k == KT - 1))
                            mm.then_inc(gu_done, 1)
                    down(qd, 0)
                    turn_hid(qd, 1)
                    with pe.If(qd + 1 < last * QUADS):
                        gather(qd + 1, 0)
                    down(qd, 1)
                    with pe.If(qd + 1 < last * QUADS):
                        gather(qd + 1, 1)
                        turn_slots(qd + 1)
                    with pe.If(qd + 1 < last * QUADS):
                        combine(qd)
                    with pe.If(qd + 1 == last * QUADS):
                        combine(qd, l + 1)


def lay_out(x, meta_tokens, norm_mix, w_in, b_if, conv_w, mh_gain, w_out, norm_ffn,
            w_group, b_group, w_router, b_router, w_gate, w_up, w_down, norm_final):
    import numpy as np

    def columns(v):
        return np.moveaxis(v.reshape(*v.shape[:-1], -1, P), -1, -2)

    h_in = columns(np.moveaxis(np.concatenate([meta_tokens, x[0]], axis=0), 0, 0))
    h_in = np.transpose(h_in, (1, 2, 0))

    def tiles(w):
        w = w.reshape(DEPTH, KT, P, -1, P)
        return np.transpose(w, (0, 3, 2, 1, 4))

    qk, vw = HEADS * P, D
    at = np.cumsum([0, qk, qk, vw, HEADS, HEADS, vw, D, D, D, D])
    q, k, v, ig, fg, gm, cx, cb, cc, gc = (w_in[:, :, a:b] for a, b in zip(at[:-1], at[1:]))
    q, k, v, gm, cx, cb, cc, gc, wo = (tiles(a) for a in (q, k, v, gm, cx, cb, cc, gc, w_out))
    order = []
    for h in range(HEADS):
        two = slice(2 * h, 2 * h + 2)
        order += [q[:, h:h + 1], k[:, h:h + 1], v[:, two], gm[:, two], cx[:, two], cc[:, two], cb[:, two], gc[:, two]]
    dense_w = np.concatenate([*order, wo], axis=1).reshape(DEPTH, DENSE, P, D)

    gate_up = np.concatenate([w_gate, w_up], axis=3)
    gate_up = gate_up.reshape(DEPTH, PAIRS, 2, KP, 2, P, 2 * D_EXPERT)
    gate_up = np.transpose(gate_up, (0, 1, 3, 2, 5, 4, 6)).reshape(DEPTH, PAIRS, GU_TILES, P, D)
    down = w_down.reshape(DEPTH, PAIRS, 2, FT, P, D)
    down = np.transpose(down, (0, 1, 3, 2, 4, 5)).reshape(DEPTH, PAIRS, 2 * FT, P, D)
    moe_w = np.concatenate([gate_up, down], axis=2).reshape(DEPTH, MOE, P, D)

    def rows(w):
        return np.transpose(w.reshape(DEPTH, KT, P, -1), (0, 2, 1, 3)).reshape(DEPTH, P, -1)

    b_gates = np.zeros((DEPTH, P, 1), np.float32)
    b_gates[:, 0:HEADS, 0] = b_if[:, :HEADS]
    b_gates[:, F_ROW:GROWS, 0] = b_if[:, HEADS:]
    b_route = np.zeros((DEPTH, P, N_ROUTE), np.float32)
    b_route[:, :, :N_GROUPS] = b_group[:, None]
    b_route[:, :, N_GROUPS:] = b_router[:, None]
    conv = np.transpose(columns(conv_w), (0, 2, 1, 3)).reshape(DEPTH, P, -1)
    params = np.concatenate([columns(norm_mix), columns(norm_ffn), columns(mh_gain), conv,
                             rows(np.concatenate([ig, fg], axis=2)),
                             rows(np.concatenate([w_group, w_router], axis=2)), b_gates, b_route], axis=2)
    params = np.transpose(params, (1, 0, 2))
    return {"h_in": h_in, "params": params, "norm_final": columns(norm_final), "dense_w": dense_w, "moe_w": moe_w}


def kernel(**inputs):
    import numpy as _np
    import concourse.bacc as _bacc
    from concourse.bass_utils import run_bass_kernel_spmd as _run

    nc = _bacc.Bacc("TRN2", target_bir_lowering=False, num_devices=1)
    arrays = {name: _np.ascontiguousarray(a) for name, a in
              lay_out(**{name: _np.asarray(a) for name, a in inputs.items()}).items()}
    args = [nc.dram_tensor(name, a.shape, F32, kind="ExternalInput").ap() for name, a in arrays.items()]
    args.append(nc.dram_tensor("out_t", (P, KT, SEQ), F32, kind="ExternalOutput").ap())
    build(nc, *args)
    r = _run(nc, [arrays], core_ids=[0])
    got = r.results[0]["out_t"]
    return _np.ascontiguousarray(_np.transpose(got, (2, 1, 0)).reshape(1, SEQ, D))
```
